# Optimizing a Trainium2 kernel written in Bass

```python
import math
import jax
import jax.numpy as jnp
from jax import lax
import numpy as np

D_MODEL = 1024
BATCH = 1
SEQ = 256
DEPTH = 2
DEC_BATCH = 1
DEC_SEQ = 512
PAST_LEN = 128

GRID_W = 64
N_MEM = 256
BLOCK = 128
EPS = 1e-6
ROPE_THETA = 10000.0
NEG_INF = -1e30

A_HEADS = 8
A_KV_HEADS = 2
A_HEAD_DIM = 64
A_GROUP = A_HEADS // A_KV_HEADS
A_Q = A_HEADS * A_HEAD_DIM
A_KV = A_KV_HEADS * A_HEAD_DIM
B_HEADS = 8
B_Q_RANK = 384
B_KV_RANK = 256
B_NOPE = 64
B_ROPE = 32
B_V = 64
B_QK = B_NOPE + B_ROPE
C_HEADS = 8
C_KV_HEADS = 2
C_HEAD_DIM = 64
C_GROUP = C_HEADS // C_KV_HEADS
C_WINDOW = 128
C_Q = C_HEADS * C_HEAD_DIM
C_KV = C_KV_HEADS * C_HEAD_DIM
X_HEADS = 4
X_HEAD_DIM = 64
X_Q = X_HEADS * X_HEAD_DIM
N_BRANCH = 4
N_EXPERTS = 16
EC_FACTOR = 2
D_EXPERT = 1024

A_WIDTH = A_Q + 2 * A_KV
B_WIDTH = B_Q_RANK + B_KV_RANK + B_ROPE
C_WIDTH = C_Q + 2 * C_KV
X_WIDTH = X_Q
IN_A = 0
IN_B = IN_A + A_WIDTH
IN_C = IN_B + B_WIDTH
IN_X = IN_C + C_WIDTH
IN_G = IN_X + X_WIDTH
IN_WIDTH = IN_G + N_BRANCH * D_MODEL
BR_A = 0
BR_B = BR_A + A_Q
BR_C = BR_B + B_HEADS * B_V
BR_X = BR_C + C_Q
BRANCH_WIDTH = BR_X + X_Q

kernel_name = 'hybrid_gated_parallel_encoder'

def rms_norm(x, g):
    xf = x.astype(jnp.float32)
    y = xf * lax.rsqrt(jnp.mean(xf * xf, axis=-1, keepdims=True) + EPS)
    return (y * g.astype(jnp.float32)).astype(x.dtype)

def rope_angles(pos, dim):
    inv = jnp.power(ROPE_THETA, -jnp.arange(0, dim, 2, dtype=jnp.float32) / dim)
    return pos.astype(jnp.float32)[:, None] * inv[None, :]

def apply_rope(x, ang):
    half = x.shape[-1] // 2
    x1, x2 = x[..., :half], x[..., half:]
    cos = jnp.cos(ang)[:, None, :].astype(x.dtype)
    sin = jnp.sin(ang)[:, None, :].astype(x.dtype)
    return jnp.concatenate([x1 * cos - x2 * sin, x1 * sin + x2 * cos], axis=-1)

def axial_rope(x, row_ang, col_ang):
    half = x.shape[-1] // 2
    return jnp.concatenate([apply_rope(x[..., :half], row_ang), apply_rope(x[..., half:], col_ang)], axis=-1)

def alibi_slopes(n_heads):
    return jnp.power(2.0, -8.0 * jnp.arange(1, n_heads + 1, dtype=jnp.float32) / n_heads)

def dense_block_attention(q, k, v, scale):
    B, S, Hkv, G, dk = q.shape
    nb = S // BLOCK
    qb = q.reshape(B, nb, BLOCK, Hkv, G, dk).transpose(1, 0, 2, 3, 4, 5)

    def one_block(qblk):
        s = jnp.einsum('bqhgd,bkhd->bhgqk', qblk, k, preferred_element_type=jnp.float32) * scale
        p = jax.nn.softmax(s, axis=-1).astype(v.dtype)
        return jnp.einsum('bhgqk,bkhd->bqhgd', p, v)

    ob = lax.map(one_block, qb)
    return ob.transpose(1, 0, 2, 3, 4, 5).reshape(B, S, Hkv, G, v.shape[-1])

def window_block_attention(q, k, v, slopes, sink, scale):
    B, S, Hkv, G, d = q.shape
    nb = S // BLOCK
    pad = [(0, 0), (BLOCK, BLOCK), (0, 0), (0, 0)]
    kp = jnp.pad(k, pad)
    vp = jnp.pad(v, pad)
    qb = q.reshape(B, nb, BLOCK, Hkv, G, d).transpose(1, 0, 2, 3, 4, 5)
    i = jnp.arange(BLOCK, dtype=jnp.int32)
    u = jnp.arange(3 * BLOCK, dtype=jnp.int32)
    rel = (u[None, :] - BLOCK) - i[:, None]
    dist = jnp.abs(rel).astype(jnp.float32)
    penalty = slopes.astype(jnp.float32)[None, :, :, None, None] * dist[None, None, None]
    sink_col = jnp.broadcast_to(sink.astype(jnp.float32)[None, :, :, None, None], (B, Hkv, G, BLOCK, 1))

    def one_block(args):
        j, qblk = args
        kb = lax.dynamic_slice_in_dim(kp, j * BLOCK, 3 * BLOCK, axis=1)
        vb = lax.dynamic_slice_in_dim(vp, j * BLOCK, 3 * BLOCK, axis=1)
        s_pos = j * BLOCK - BLOCK + u
        valid = (jnp.abs(rel) <= C_WINDOW) & ((s_pos >= 0) & (s_pos < S))[None, :]
        s = jnp.einsum('bqhgd,bkhd->bhgqk', qblk, kb, preferred_element_type=jnp.float32) * scale - penalty
        s = jnp.where(valid[None, None, None], s, NEG_INF)
        p = jax.nn.softmax(jnp.concatenate([s, sink_col], axis=-1), axis=-1)[..., :-1].astype(v.dtype)
        return jnp.einsum('bhgqk,bkhd->bqhgd', p, vb)

    ob = lax.map(one_block, (jnp.arange(nb, dtype=jnp.int32), qb))
    return ob.transpose(1, 0, 2, 3, 4, 5).reshape(B, S, Hkv, G, d)

def mixer_a(z, row_ang, col_ang, q_g, k_g):
    B, S, _ = z.shape
    q = z[..., :A_Q].reshape(B, S, A_HEADS, A_HEAD_DIM)
    k = z[..., A_Q:A_Q + A_KV].reshape(B, S, A_KV_HEADS, A_HEAD_DIM)
    v = z[..., A_Q + A_KV:].reshape(B, S, A_KV_HEADS, A_HEAD_DIM)
    q = axial_rope(rms_norm(q, q_g), row_ang, col_ang)
    k = axial_rope(rms_norm(k, k_g), row_ang, col_ang)
    q = q.reshape(B, S, A_KV_HEADS, A_GROUP, A_HEAD_DIM)
    o = dense_block_attention(q, k, v, A_HEAD_DIM ** -0.5)
    return o.reshape(B, S, A_Q)

def mixer_b(z, seq_ang, q_a_g, w_q_b, kv_a_g, w_kv_b, q_g, k_g):
    B, S, _ = z.shape
    c_q = z[..., :B_Q_RANK]
    c_kv = z[..., B_Q_RANK:B_Q_RANK + B_KV_RANK]
    k_rope = z[..., B_Q_RANK + B_KV_RANK:]
    q = (rms_norm(c_q, q_a_g) @ w_q_b).reshape(B, S, B_HEADS, B_QK)
    kv = (rms_norm(c_kv, kv_a_g) @ w_kv_b).reshape(B, S, B_HEADS, B_NOPE + B_V)
    k_nope, v = kv[..., :B_NOPE], kv[..., B_NOPE:]
    k = jnp.concatenate([k_nope, jnp.broadcast_to(k_rope[:, :, None, :], (B, S, B_HEADS, B_ROPE))], axis=-1)
    q = rms_norm(q, q_g)
    k = rms_norm(k, k_g)
    q = jnp.concatenate([q[..., :B_NOPE], apply_rope(q[..., B_NOPE:], seq_ang)], axis=-1)
    k = jnp.concatenate([k[..., :B_NOPE], apply_rope(k[..., B_NOPE:], seq_ang)], axis=-1)
    o = dense_block_attention(q[:, :, :, None, :], k, v, B_QK ** -0.5)
    return o.reshape(B, S, B_HEADS * B_V)

def mixer_c(z, slopes, sink, q_g, k_g):
    B, S, _ = z.shape
    q = rms_norm(z[..., :C_Q].reshape(B, S, C_HEADS, C_HEAD_DIM), q_g)
    k = rms_norm(z[..., C_Q:C_Q + C_KV].reshape(B, S, C_KV_HEADS, C_HEAD_DIM), k_g)
    v = z[..., C_Q + C_KV:].reshape(B, S, C_KV_HEADS, C_HEAD_DIM)
    q = q.reshape(B, S, C_KV_HEADS, C_GROUP, C_HEAD_DIM)
    o = window_block_attention(q, k, v, slopes, sink, C_HEAD_DIM ** -0.5)
    return o.reshape(B, S, C_Q)

def memory_cross_attention(zq, mem, mem_g, w_mem_kv, q_g, k_g):
    B, S, _ = zq.shape
    q = rms_norm(zq.reshape(B, S, X_HEADS, X_HEAD_DIM), q_g)
    kv = rms_norm(mem, mem_g) @ w_mem_kv
    k = rms_norm(kv[..., :X_Q].reshape(B, N_MEM, X_HEADS, X_HEAD_DIM), k_g)
    v = kv[..., X_Q:].reshape(B, N_MEM, X_HEADS, X_HEAD_DIM)
    s = jnp.einsum('bqhd,bkhd->bhqk', q, k, preferred_element_type=jnp.float32) * (X_HEAD_DIM ** -0.5)
    p = jax.nn.softmax(s, axis=-1).astype(v.dtype)
    return jnp.einsum('bhqk,bkhd->bqhd', p, v).reshape(B, S, X_Q)

def expert_choice_moe(h, w_router, w_gate_up, w_down):
    B, S, D = h.shape
    n = B * S
    cap = EC_FACTOR * n // N_EXPERTS
    xt = h.reshape(n, D)
    aff = jax.nn.softmax((xt @ w_router).astype(jnp.float32), axis=-1)
    gate, idx = lax.top_k(aff.T, cap)
    xs = xt[idx]
    gu = jnp.einsum('ecd,edf->ecf', xs, w_gate_up)
    g, u = gu[..., :D_EXPERT], gu[..., D_EXPERT:]
    y = jnp.einsum('ecf,efd->ecd', jax.nn.silu(g) * u, w_down) * gate[..., None].astype(h.dtype)
    out = jnp.zeros_like(xt).at[idx.reshape(-1)].add(y.reshape(-1, D))
    return out.reshape(B, S, D)

def encoder_trunk(x, mem, norm1_g, w_in, a_q_norm, a_k_norm, b_q_a_norm, b_w_q_b, b_kv_a_norm, b_w_kv_b,
                  b_q_norm, b_k_norm, c_q_norm, c_k_norm, c_sink, x_q_norm, x_k_norm, mem_norm_g, w_mem_kv,
                  w_branch, w_out, norm2_g, w_router, w_gate_up, w_down):
    B, S, D = x.shape
    rows = S // GRID_W
    row_idx = jnp.repeat(jnp.arange(rows, dtype=jnp.int32), GRID_W)
    col_idx = jnp.tile(jnp.arange(GRID_W, dtype=jnp.int32), rows)
    tok_idx = jnp.arange(S, dtype=jnp.int32)
    row_ang = rope_angles(row_idx, A_HEAD_DIM // 2)
    col_ang = rope_angles(col_idx, A_HEAD_DIM // 2)
    seq_ang = rope_angles(tok_idx, B_ROPE)
    slopes = alibi_slopes(C_HEADS).reshape(C_KV_HEADS, C_GROUP)
    for l in range(DEPTH):
        h = rms_norm(x, norm1_g[l])
        z = h @ w_in[l]
        oa = mixer_a(z[..., IN_A:IN_B], row_ang, col_ang, a_q_norm[l], a_k_norm[l])
        ob = mixer_b(z[..., IN_B:IN_C], seq_ang, b_q_a_norm[l], b_w_q_b[l], b_kv_a_norm[l], b_w_kv_b[l],
                     b_q_norm[l], b_k_norm[l])
        oc = mixer_c(z[..., IN_C:IN_X], slopes, c_sink[l].reshape(C_KV_HEADS, C_GROUP), c_q_norm[l], c_k_norm[l])
        ox = memory_cross_attention(z[..., IN_X:IN_G], mem, mem_norm_g[l], w_mem_kv[l], x_q_norm[l], x_k_norm[l])
        gates = jax.nn.sigmoid(z[..., IN_G:].astype(jnp.float32)).astype(x.dtype).reshape(B, S, N_BRANCH, D)
        wb = w_branch[l]
        merged = (gates[:, :, 0] * (oa @ wb[BR_A:BR_B])
                  + gates[:, :, 1] * (ob @ wb[BR_B:BR_C])
                  + gates[:, :, 2] * (oc @ wb[BR_C:BR_X])
                  + gates[:, :, 3] * (ox @ wb[BR_X:]))
        x = x + merged @ w_out[l]
        x = x + expert_choice_moe(rms_norm(x, norm2_g[l]), w_router[l], w_gate_up[l], w_down[l])
    return x

def setup_inputs(seed: int = 0) -> dict:
    key = jax.random.key(seed)
    ks = jax.random.split(key, 28)
    f32 = jnp.float32

    def nrm(k, shape, fan_in):
        return jax.random.normal(k, shape, f32) * (fan_in ** -0.5)

    def gain(k, shape):
        return 1.0 + 0.01 * jax.random.normal(k, shape, f32)

    return {
        'x_prompt': jax.random.normal(ks[0], (BATCH, SEQ, D_MODEL), f32),
        'x_sample': jax.random.normal(ks[1], (DEC_BATCH, DEC_SEQ, D_MODEL), f32),
        'mem_prompt': jax.random.normal(ks[2], (BATCH, N_MEM, D_MODEL), f32),
        'mem_sample': jax.random.normal(ks[3], (DEC_BATCH, N_MEM, D_MODEL), f32),
        'norm1_g': gain(ks[4], (DEPTH, D_MODEL)),
        'w_in': nrm(ks[5], (DEPTH, D_MODEL, IN_WIDTH), D_MODEL),
        'a_q_norm': gain(ks[6], (DEPTH, A_HEAD_DIM)),
        'a_k_norm': gain(ks[7], (DEPTH, A_HEAD_DIM)),
        'b_q_a_norm': gain(ks[8], (DEPTH, B_Q_RANK)),
        'b_w_q_b': nrm(ks[9], (DEPTH, B_Q_RANK, B_HEADS * B_QK), B_Q_RANK),
        'b_kv_a_norm': gain(ks[10], (DEPTH, B_KV_RANK)),
        'b_w_kv_b': nrm(ks[11], (DEPTH, B_KV_RANK, B_HEADS * (B_NOPE + B_V)), B_KV_RANK),
        'b_q_norm': gain(ks[12], (DEPTH, B_QK)),
        'b_k_norm': gain(ks[13], (DEPTH, B_QK)),
        'c_q_norm': gain(ks[14], (DEPTH, C_HEAD_DIM)),
        'c_k_norm': gain(ks[15], (DEPTH, C_HEAD_DIM)),
        'c_sink': 0.5 * jax.random.normal(ks[16], (DEPTH, C_HEADS), f32),
        'x_q_norm': gain(ks[17], (DEPTH, X_HEAD_DIM)),
        'x_k_norm': gain(ks[18], (DEPTH, X_HEAD_DIM)),
        'mem_norm_g': gain(ks[19], (DEPTH, D_MODEL)),
        'w_mem_kv': nrm(ks[20], (DEPTH, D_MODEL, 2 * X_Q), D_MODEL),
        'w_branch': nrm(ks[21], (DEPTH, BRANCH_WIDTH, D_MODEL), A_Q),
        'w_out': nrm(ks[22], (DEPTH, D_MODEL, D_MODEL), D_MODEL),
        'norm2_g': gain(ks[23], (DEPTH, D_MODEL)),
        'w_router': nrm(ks[24], (DEPTH, D_MODEL, N_EXPERTS), D_MODEL),
        'w_gate_up': nrm(ks[25], (DEPTH, N_EXPERTS, D_MODEL, 2 * D_EXPERT), D_MODEL),
        'w_down': nrm(ks[26], (DEPTH, N_EXPERTS, D_EXPERT, D_MODEL), D_EXPERT),
    }

def reference(x_prompt, x_sample, mem_prompt, mem_sample, norm1_g, w_in, a_q_norm, a_k_norm, b_q_a_norm,
              b_w_q_b, b_kv_a_norm, b_w_kv_b, b_q_norm, b_k_norm, c_q_norm, c_k_norm, c_sink, x_q_norm,
              x_k_norm, mem_norm_g, w_mem_kv, w_branch, w_out, norm2_g, w_router, w_gate_up, w_down):
    y_prompt = encoder_trunk(x_prompt, mem_prompt, norm1_g, w_in, a_q_norm, a_k_norm, b_q_a_norm, b_w_q_b,
                             b_kv_a_norm, b_w_kv_b, b_q_norm, b_k_norm, c_q_norm, c_k_norm, c_sink, x_q_norm,
                             x_k_norm, mem_norm_g, w_mem_kv, w_branch, w_out, norm2_g, w_router, w_gate_up, w_down)
    y_sample = encoder_trunk(x_sample, mem_sample, norm1_g, w_in, a_q_norm, a_k_norm, b_q_a_norm, b_w_q_b,
                             b_kv_a_norm, b_w_kv_b, b_q_norm, b_k_norm, c_q_norm, c_k_norm, c_sink, x_q_norm,
                             x_k_norm, mem_norm_g, w_mem_kv, w_branch, w_out, norm2_g, w_router, w_gate_up, w_down)
    return (y_prompt, y_sample)


_drawn_inputs = setup_inputs


def setup_inputs(seed=0):
    import zlib

    import numpy as np

    out = dict(_drawn_inputs(seed))
    spreads = {}
    factors = {'norm1_g': 4.586,
     'a_q_norm': 5.762,
     'a_k_norm': 8.0,
     'b_q_a_norm': 8.0,
     'b_kv_a_norm': 6.973,
     'b_q_norm': 8.0,
     'b_k_norm': 8.0,
     'c_q_norm': 5.021,
     'c_k_norm': 7.01,
     'c_sink': 2.941,
     'x_q_norm': 7.679,
     'x_k_norm': 8.0,
     'mem_norm_g': 8.0,
     'norm2_g': 3.176}
    for name, (base, spread) in spreads.items():
        noise = np.random.default_rng([zlib.crc32(name.encode()), seed]).standard_normal(out[name].shape)
        drawn = base * np.exp(spread * noise) if base else spread * noise
        out[name] = jnp.asarray(drawn.astype(out[name].dtype))
    for name, factor in factors.items():
        out[name] = (out[name] * factor).astype(out[name].dtype)
    return out
```

```python
from contextlib import ExitStack

import concourse.bass as bass
from concourse import mybir

F32 = mybir.dt.float32
F32R = mybir.dt.float32r
U32 = mybir.dt.uint32
ALU = mybir.AluOpType
ACT = mybir.ActivationFunctionType
AX = mybir.AxisListType

P = 128
DEPTH = 2
D = 1024
KD = D // P
SEQS = [(0, 2), (2, 4)]
NT = 6
NTOK = NT * P
MT = 4
HD = 64
QR, KVR, ROPE = 384, 256, 32
BQK = HD + ROPE
EPS = 1e-6
NE = 16
CAPS = [32, 64]
CAP = sum(CAPS)
DE = 1024

IN_A, IN_B, IN_C, IN_X, IN_G = 0, 768, 1440, 2208, 2464

CW = 256
SLOT = KD * CW
Z_CHUNKS = {
    "A": [(2, 0, 256), (3, 256, 256), (4, 512, 256)],
    "B": [(5, 0, 256), (6, 256, 256), (7, 512, 160)],
    "C": [(8, 0, 256), (9, 256, 256), (10, 512, 256)],
    "X": [(11, 0, 256)],
}
Z_BASE = {"A": IN_A, "B": IN_B, "C": IN_C, "X": IN_X}
Z_GROUP = {"A": 0, "B": 18, "C": 36, "X": 54}
GATE0 = 12
NGEMM = 28
MPOS = 12
NCHUNK = NGEMM + NE * MPOS
MSLOTS = 6
POOL_EVERY = 3
LO_PER_E = MPOS - MPOS // POOL_EVERY

LEAD = 16


class Signal:

    def __init__(self, sem, n, unit=1, lead=LEAD):
        self.sem, self.n, self.unit, self.lead = sem, n, unit, lead

    def start(self, eng):
        if self.lead:
            eng.sem_inc(self.sem, self.lead * self.unit)

    def at(self, layer, k):
        return (layer * self.n + k + 1 + self.lead) * self.unit


class Branch:
    def __init__(self, name, its, heads, rows, unit0, hs0, pair0, prep0, nprep):
        self.name, self.its, self.heads, self.rows = name, its, heads, rows
        self.unit0, self.hs0, self.pair0, self.prep0, self.nprep = unit0, hs0, pair0, prep0, nprep
        self.units = []
        for pair in range(heads // 2):
            for s, (t0, n) in enumerate(SEQS):
                for h in (2 * pair, 2 * pair + 1):
                    for t in range(t0, t0 + n):
                        self.units.append((h, s, t, t == t0 + n - 1))

    def hs(self, u):
        return sum(last for *_, last in self.units[:u])

    def nkt(self, s):
        return 2 if self.name == "X" else SEQS[s][1]

    def key_tile(self, s):
        return 2 * s if self.name == "X" else SEQS[s][0]

    def q(self, QT, h, t):
        c = slice(t * P, (t + 1) * P)
        if self.name == "B":
            return QT[0:BQK, h, c]
        return QT[(h % 2) * HD:(h % 2 + 1) * HD, h // 2, c]

    def k(self, KT, h, s):
        c = slice(self.key_tile(s) * P, (self.key_tile(s) + self.nkt(s)) * P)
        if self.name == "B":
            return KT[0:BQK, h, c]
        return KT[(h % 2) * HD:(h % 2 + 1) * HD, 0, c]

    def v(self, VS, h, s, kt):
        c = 0 if self.name in "AC" else h * HD
        return VS[:, self.key_tile(s) + kt, c:c + HD]


BR = {
    "A": Branch("A", 2, 4, HD, 0, 0, 0, 0, 6),
    "B": Branch("B", 4, 2, BQK, 48, 16, 4, 22, 8),
    "C": Branch("C", 2, 4, HD, 96, 32, 8, 54, 6),
    "X": Branch("X", 2, 2, HD, 144, 48, 12, 66, 4),
}
B_CPREP0 = 12
STAGE0 = {"A": 0, "C": 2, "X": 4}
PREP_A, PREP_BC, PREP_BP, PREP_C, PREP_X, NPREP = 0, 1, 2, 6, 7, 8


def build(nc, x_in, mem_in, w, gains, tables, y_prompt, y_sample):
    ctx = ExitStack()
    with ctx:
        def sb(name, shape, dt=F32):
            return ctx.enter_context(nc.sbuf_tensor(name, shape, dt))

        signals = []

        def sig(name, n, unit=1, lead=LEAD):
            s = Signal(ctx.enter_context(nc.semaphore(name)), n, unit, lead)
            signals.append(s)
            return s

        def dma_sig(name, n):
            return sig(name, n, 16)

        x_acc = nc.dram_tensor("x_acc", [NTOK, D], F32)
        h_rows = nc.dram_tensor("h_rows", [NTOK, D], F32)
        o_rows = nc.dram_tensor("o_rows", [14 * P, NTOK], F32)

        wraw = sb("wraw", [P, 2, SLOT])
        whi = sb("whi", [P, 2, SLOT], F32R)
        wlo = sb("wlo", [P, 2, SLOT], F32R)
        mkv = sb("mkv", [P, MT, 2 * 4 * HD])
        ident = sb("ident", [P, P])
        ones = sb("ones", [P, P])
        eps_t = sb("eps_t", [P, 1])
        cosA = sb("cosA", [P, NT, HD])
        sinA = sb("sinA", [P, NT, HD])
        cosB = sb("cosB", [P, 2 * NT, ROPE])
        sinB = sb("sinB", [P, 2 * NT, ROPE])
        ndist = sb("ndist", [P, 7 * P])
        slopes = sb("slopes", [P, 8])
        sinks = sb("sinks", [P, 8])
        g_head = sb("g_head", [P, 6, HD])
        g_b = sb("g_b", [P, 2, BQK])
        g_bc = sb("g_bc", [P, QR + KVR])
        stat = sb("stat", [P, 64])
        row_ss = sb("row_ss", [P, 2])
        row_rt = sb("row_rt", [P, 2])
        nmax = sb("nmax", [P, 4])
        nraw = sb("nraw", [P, 4])
        psums = sb("psums", [P, 4])
        esink = sb("esink", [P, 4])
        prec = sb("prec", [P, 4])
        it_slope = sb("it_slope", [P, 4])
        it_sink = sb("it_sink", [P, 4])
        it_nsink = sb("it_nsink", [P, 4])

        sgb = sb("sgb", [P, 2, CW])
        gpb = sb("gpb", [P, 2, CW])
        wr = sb("wr", [P, KD, NE])
        lg = sb("lg", [P, NT, NE])
        rst = sb("rst", [P, NT, 4])
        val = sb("val", [NE, CAP])
        idu = sb("idu", [NE, CAP], U32)
        idf = sb("idf", [NE, CAP])
        valT = sb("valT", [CAP, NE])
        idxT = sb("idxT", [CAP, NE], U32)
        ig = sb("ig", [CAP, 1], U32)
        isc = sb("isc", [CAP, 1], U32)

        def region(name, size):
            slab = sb(name, [P, size // 4])
            start = nc.sbuf_base - size

            def plan():
                at = [0]

                def take(name, shape, dt=F32):
                    n = 4
                    for m in shape[1:]:
                        n *= m
                    t = nc.alloc_sbuf_tensor_at(name, shape, dt, offset=start + at[0])
                    at[0] += n
                    assert at[0] <= size, (name, at[0], size)
                    return t
                return take
            return plan

        rows_region = region("rows_region", 2 * KD * NTOK * 4)
        arena = region("arena", 88 * 1024)

        take = rows_region()
        hT_hi = take("hT_hi", [P, KD, NTOK], F32R)
        hT_lo = take("hT_lo", [P, KD, NTOK], F32R)
        take = rows_region()
        X2 = take("X2", [P, NT, D])
        g_n2 = take("g_n2", [P, D])
        H2 = take("H2", [P, 2, D])
        nscr2 = take("nscr2", [P, D])
        H2T = take("H2T", [P, KD, P])
        affT = take("affT", [NE, NTOK])
        take = rows_region()
        XS = take("XS", [CAP, D])
        xsT_hi = take("xsT_hi", [P, KD, CAP], F32R)
        xsT_lo = take("xsT_lo", [P, KD, CAP], F32R)
        sg = take("sg", [CAP, 2, 512])
        act_s = take("act_s", [CAP, DE])
        aT_hi = take("aT_hi", [P, KD, CAP], F32R)
        aT_lo = take("aT_lo", [P, KD, CAP], F32R)
        YS = take("YS", [CAP, D])
        take = arena()
        xin = take("xin", [P, 2, D])
        g_mem = take("g_mem", [P, D])
        g_n1 = take("g_n1", [P, D])
        nscr = take("nscr", [P, 2, D])
        take = arena()
        Z = take("Z", [P, NT, 768])
        QS = take("QS", [P, NT * 256])
        KS = take("KS", [P, NT * 2 * BQK])
        VS = take("VS", [P, NT, 2 * HD])
        QT = take("QT", [P, 2, NTOK])
        KT = take("KT", [P, 2, NTOK])
        PR = take("PR", [P, 3, 512])
        PT = take("PT", [P, 2, 4, 512])
        OS = take("OS", [P, NTOK])
        cT = take("cT", [P, 5, NTOK])
        wqp = take("wqp", [P, 3, 2 * BQK])
        wkvp = take("wkvp", [P, 2, 4 * HD])
        take = arena()
        oT = take("oT", [P, 14, NTOK])
        mg = take("mg", [P, NT, CW])
        wdir = take("wdir", [P, 2, SLOT])
        mT = take("mT", [P, KD, NTOK])
        take = arena()
        mraw = take("mraw", [P, MSLOTS, SLOT])

        bank = [ctx.enter_context(nc.psum_tensor(f"bank{i}", [P, 512], F32)) for i in range(8)]

        s_x0 = ctx.enter_context(nc.semaphore("x0_stored"))
        s_tab = ctx.enter_context(nc.semaphore("tables_loaded"))
        s_cst = ctx.enter_context(nc.semaphore("consts_made"))
        passed = {e: ctx.enter_context(nc.semaphore(f"passed_{e}")) for e in ("act", "pool", "pe", "dve", "sp")}
        s_out = ctx.enter_context(nc.semaphore("outputs_stored"))
        gains_in = dma_sig("gains_in", 12)
        krope_in = sig("krope_in", 4)
        g2_in = dma_sig("g2_in", 2)
        gn2_in = dma_sig("gn2_in", 1)
        w_in_slot = [dma_sig(f"w_in_slot{i}", NGEMM // 2) for i in range(2)]
        m_in_slot = [dma_sig(f"m_in_slot{i}", NE * MPOS // MSLOTS) for i in range(MSLOTS)]
        hi_made = sig("hi_made", NCHUNK)
        lo_made = sig("lo_made", NGEMM + LO_PER_E * NE)
        lo_pool = sig("lo_pool", (MPOS - LO_PER_E) * NE)
        xin_in = [dma_sig(f"xin_in{i}", 5) for i in range(2)]
        row_root = sig("row_root", 10)
        row_normed = sig("row_normed", 10)
        row_turned = sig("row_turned", 10)
        row_hi = sig("row_hi", 10)
        row_lo = sig("row_lo", 10)
        mem_mm = sig("mem_mm", 8)
        mem_ev = sig("mem_ev", 8)
        z_mm = sig("z_mm", 60)
        z_ev = sig("z_ev", 60)
        pq_sq = sig("pq_sq", NPREP)
        pq_sum = sig("pq_sum", NPREP)
        pq_root = sig("pq_root", NPREP)
        pq_done = sig("pq_done", NPREP)
        staged = sig("staged", 6)
        prep_t = sig("prep_t", 74)
        prep_ev = sig("prep_ev", 74)
        bw_in = [dma_sig(f"bw_in{i}", 4) for i in range(2)]
        bp_mm = sig("bp_mm", 24)
        bp_ev = sig("bp_ev", 24)
        sc_mm = sig("sc_mm", 168)
        sc_max = sig("sc_max", 168)
        p_exp = sig("p_exp", 168)
        p_rec = sig("p_rec", 168)
        p_norm = sig("p_norm", 168)
        p_turn = sig("p_turn", 168)
        p_ev = sig("p_ev", 168)
        pv_mm = sig("pv_mm", 56)
        o_ev = sig("o_ev", 28)
        o_out = dma_sig("o_out", 14)
        o_in = dma_sig("o_in", 1)
        d_in = [dma_sig(f"d_in{i}", 6) for i in range(2)]
        gate_mm = sig("gate_mm", 96)
        gate_sg = sig("gate_sg", 96)
        gate_mg = sig("gate_mg", 96)
        mg_t = sig("mg_t", 16)
        mg_ev = sig("mg_ev", 16)
        x_in2 = dma_sig("x_in2", 1)
        out_mm = sig("out_mm", 24)
        out_ev = sig("out_ev", 24)
        r2_root = sig("r2_root", 6)
        r2_normed = sig("r2_normed", 6)
        x_out = dma_sig("x_out", 6)
        h_out = [dma_sig(f"h_out{i}", 3) for i in range(2)]
        r2_turn = sig("r2_turn", 12)
        r2_ev = sig("r2_ev", 12)
        rl_mm = sig("rl_mm", 6)
        rl_max = sig("rl_max", 6)
        rl_exp = sig("rl_exp", 6)
        rl_aff = sig("rl_aff", 6)
        aff_t = sig("aff_t", 1)
        top_done = sig("top_done", 1)
        top_t = sig("top_t", 1)
        top_ev = sig("top_ev", 1)
        ig_ok = sig("ig_ok", 2 * NE)
        xs_in = sig("xs_in", NE, 16, 0)
        xs_t = sig("xs_t", 2 * NE)
        xs_hi = sig("xs_hi", 2 * NE)
        xs_lo = sig("xs_lo", 2 * NE)
        m_used = sig("m_used", MPOS * NE)
        silu_ok = sig("silu_ok", 2 * NE)
        act_ok = sig("act_ok", 2 * NE)
        a_t = sig("a_t", 2 * NE)
        a_hi = sig("a_hi", 2 * NE)
        a_lo = sig("a_lo", 2 * NE)
        y_ev = sig("y_ev", 2 * NE)
        y_out = sig("y_out", NE, 16, 0)
        y_done = sig("y_done", NE)

        def m_lo_index(e, pos):
            return NGEMM + e * LO_PER_E + pos - pos // POOL_EVERY - 1

        def kpn(ap):
            return ap.rearrange("o (k p) n -> (o p) k n", p=P)

        def lay(t, l):
            return t[bass.ds(l, 1)]

        block = ctx.enter_context(nc.Block())

        @block.sync
        def _(sp):
            for t, src in ((cosA, "cosA"), (sinA, "sinA"), (cosB, "cosB"), (sinB, "sinB"), (ndist, "ndist"),
                           (slopes, "slopes")):
                sp.dma_start(t[:], tables[src]).then_inc(s_tab, 16)
            sp.dma_start(x_acc[:, :], x_in).then_inc(s_x0, 16)

            def load_w(l, j, src, width, rows=KD):
                k = j - 2
                sp.wait_ge(lo_made.sem, lo_made.at(l, k))
                sp.dma_start(wraw[:, j % 2, 0:rows * width].rearrange("p (k n) -> p k n", n=width), src)\
                  .then_inc(w_in_slot[j % 2].sem, 16)

            def load_z(l, name, n):
                j, c, width = Z_CHUNKS[name][n]
                c += Z_BASE[name]
                load_w(l, j, kpn(lay(w["w_in"], l)[:, :, c:c + width]), width)

            def store_pairs(l, br, it):
                for pr in range(br.heads // 2):
                    n = it * (br.heads // 2) + pr + br.pair0
                    row = sp.snap(n * P)
                    sp.wait_ge(o_ev.sem, o_ev.at(l, 2 * n + 1))
                    sp.dma_start(o_rows[bass.ds(row, P), :], OS[:]).then_inc(o_out.sem, 16)

            with sp.Fori(0, DEPTH) as l:
                sp.wait_ge(lo_made.sem, lo_made.at(l, -1))
                sp.wait_ge(y_done.sem, y_done.at(l, -1))
                for t, name in ((g_mem[:], "mem_norm_g"), (g_n1[:], "norm1_g"), (g_head[:, 0, :], "a_q_norm"),
                                (g_head[:, 1, :], "a_k_norm"), (g_head[:, 2, :], "c_q_norm"),
                                (g_head[:, 3, :], "c_k_norm"), (g_head[:, 4, :], "x_q_norm"),
                                (g_head[:, 5, :], "x_k_norm"), (g_b[:, 0, :], "b_q_norm"),
                                (g_b[:, 1, :], "b_k_norm"), (g_bc[:, 0:QR], "b_q_a_norm"),
                                (g_bc[:, QR:QR + KVR], "b_kv_a_norm")):
                    sp.dma_start(t, gains[name][bass.ds(l, 1), :].to_broadcast([P, t.shape[-1]]))\
                      .then_inc(gains_in.sem, 16)
                sp.dma_start(sinks[:], gains["c_sink"][bass.ds(l, 1), :].to_broadcast([P, 8])).then_inc(g2_in.sem, 16)
                sp.dma_start(wr[:], kpn(lay(w["w_router"], l))).then_inc(g2_in.sem, 16)
                for c in range(2):
                    load_w(l, c, kpn(lay(w["w_mem_kv"], l)[:, :, c * CW:(c + 1) * CW]), CW)
                with sp.Fori(0, MT // 2) as it:
                    for b in range(2):
                        row = sp.snap((it * 2 + b) * P)
                        sp.wait_ge(row_turned.sem, row_turned.at(l, it * 2 + b - 2))
                        sp.dma_start(xin[:, b, :], mem_in[bass.ds(row, P), :]).then_inc(xin_in[b].sem, 16)
                load_z(l, "A", 0)
                sp.wait_ge(s_x0, 16)
                with sp.Fori(0, NT // 2) as it:
                    for b in range(2):
                        row = sp.snap((it * 2 + b) * P)
                        sp.wait_ge(row_turned.sem, row_turned.at(l, it * 2 + b + MT - 2))
                        sp.dma_start(xin[:, b, :], x_acc[bass.ds(row, P), :]).then_inc(xin_in[b].sem, 16)
                load_z(l, "A", 1)
                load_z(l, "A", 2)
                load_z(l, "B", 0)
                load_z(l, "B", 1)
                with sp.Fori(0, BR["A"].its) as it:
                    store_pairs(l, BR["A"], it)
                load_z(l, "B", 2)
                load_z(l, "C", 0)
                load_z(l, "C", 1)
                with sp.Fori(0, BR["B"].its) as it:
                    qc = sp.snap(it * 2 * BQK)
                    kc = sp.snap(it * 4 * HD)
                    sp.wait_ge(bp_mm.sem, bp_mm.at(l, it * NT - 1))
                    sp.dma_start(wqp[:], kpn(lay(w["b_w_q_b"], l)[:, :, bass.ds(qc, 2 * BQK)])).then_inc(bw_in[0].sem, 16)
                    sp.dma_start(wkvp[:], kpn(lay(w["b_w_kv_b"], l)[:, :, bass.ds(kc, 4 * HD)])).then_inc(bw_in[1].sem, 16)
                    store_pairs(l, BR["B"], it)
                load_z(l, "C", 2)
                load_z(l, "X", 0)
                with sp.Fori(0, BR["C"].its) as it:
                    store_pairs(l, BR["C"], it)

                def load_gate(n, b):
                    j = GATE0 + 4 * n + b
                    slot = b % 2
                    c = sp.snap(n * CW + IN_G + b * D)
                    sp.wait_ge(lo_made.sem, lo_made.at(l, j - 2))
                    sp.dma_start(wraw[:, slot, :].rearrange("p (k n) -> p k n", n=CW),
                                 kpn(lay(w["w_in"], l)[:, :, bass.ds(c, CW)])).then_inc(w_in_slot[slot].sem, 16)

                load_gate(0, 0)
                load_gate(0, 1)
                with sp.Fori(0, BR["X"].its) as it:
                    store_pairs(l, BR["X"], it)
                sp.wait_ge(o_out.sem, o_out.at(l, 13))
                sp.dma_start(oT[:], o_rows[:, :].rearrange("(k p) n -> p k n", p=P)).then_inc(o_in.sem, 16)

                def load_direct(before, k0, slot, rows, k):
                    sp.wait_ge(before.sem, before.at(l, k0))
                    sp.dma_start(wdir[:, slot, 0:k * CW].rearrange("p (k n) -> p k n", n=CW), rows)\
                      .then_inc(d_in[slot].sem, 16)

                def gate_loads(n, last):
                    c = sp.snap(n * CW)
                    load_direct(gate_mm, n * 24 - 13, 0, kpn(lay(w["w_branch"], l)[:, 0:1024, bass.ds(c, CW)]), 8)
                    for b in range(2):
                        load_gate(n, b + 2)
                    c = sp.snap(n * CW)
                    load_direct(gate_mm, n * 24 - 1, 1, kpn(lay(w["w_branch"], l)[:, 1024:1792, bass.ds(c, CW)]), 6)
                    if not last:
                        for b in range(2):
                            load_gate(n + 1, b)

                with sp.Fori(0, 3) as n:
                    gate_loads(n, False)
                gate_loads(3, True)
                for c in range(2):
                    load_direct(gate_mm, 83 + 12 * c, c, kpn(lay(w["w_out"], l)[:, :, c * CW:(c + 1) * CW]), 8)
                sp.wait_ge(gate_mm.sem, gate_mm.at(l, 95))
                sp.dma_start(X2[:], x_acc[:, :].rearrange("(t p) n -> p t n", p=P)).then_inc(x_in2.sem, 16)
                sp.dma_start(g_n2[:], gains["norm2_g"][bass.ds(l, 1), :].to_broadcast([P, D])).then_inc(gn2_in.sem, 16)

                def m_src(e, pos):
                    if pos < 8:
                        col = [0, DE, 512, DE + 512][pos // 2]
                        t = w["w_gate_up"][bass.ds(e, 1), (pos % 2) * 512:(pos % 2 + 1) * 512, col:col + 512]
                    else:
                        r, c = (pos - 8) // 2 * 512, (pos - 8) % 2 * 512
                        t = w["w_down"][bass.ds(e, 1), r:r + 512, c:c + 512]
                    return kpn(t)

                def load_m(e, pos):
                    ex = sp.snap(l * NE + e)
                    sp.dma_start(mraw[:, pos % MSLOTS, :].rearrange("p (k n) -> p k n", n=512), m_src(ex, pos))\
                      .then_inc(m_in_slot[pos % MSLOTS].sem, 16)

                sp.wait_ge(mg_t.sem, mg_t.at(l, 15))
                for pos in range(MSLOTS):
                    load_m(0, pos)
                for c in range(2, 4):
                    load_direct(out_mm, 6 * c - 7, c % 2, kpn(lay(w["w_out"], l)[:, :, c * CW:(c + 1) * CW]), 8)

                def m_loads(e, last):
                    for pos in range(MPOS):
                        if pos < MPOS - MSLOTS:
                            ex = sp.snap(l * NE + e)
                            if pos % POOL_EVERY == 0:
                                sp.wait_ge(lo_pool.sem, lo_pool.at(l, e * (MPOS // POOL_EVERY) + pos // POOL_EVERY))
                            else:
                                sp.wait_ge(lo_made.sem, lo_made.at(l, m_lo_index(e, pos)))
                            sp.dma_start(mraw[:, pos % MSLOTS, :].rearrange("p (k n) -> p k n", n=512),
                                         m_src(ex, pos + MSLOTS)).then_inc(m_in_slot[pos % MSLOTS].sem, 16)
                        elif not last:
                            ex = sp.snap(l * NE + e + 1)
                            if pos % POOL_EVERY == 0:
                                sp.wait_ge(lo_pool.sem, lo_pool.at(l, e * (MPOS // POOL_EVERY) + pos // POOL_EVERY))
                            else:
                                sp.wait_ge(lo_made.sem, lo_made.at(l, m_lo_index(e, pos)))
                            sp.dma_start(mraw[:, pos % MSLOTS, :].rearrange("p (k n) -> p k n", n=512),
                                         m_src(ex, pos + MSLOTS - MPOS)).then_inc(m_in_slot[pos % MSLOTS].sem, 16)

                for t in range(NT):
                    sp.wait_ge(r2_normed.sem, r2_normed.at(l, t))
                    sp.dma_start(x_acc[t * P:(t + 1) * P, :], X2[:, t, :]).then_inc(x_out.sem, 16)
                    sp.dma_start(h_rows[t * P:(t + 1) * P, :], H2[:, t % 2, :]).then_inc(h_out[t % 2].sem, 16)
                with sp.Fori(0, NE - 1) as e:
                    m_loads(e, False)
                m_loads(NE - 1, True)

            sp.wait_ge(y_done.sem, y_done.at(DEPTH - 1, NE - 1))
            sp.dma_start(y_prompt, x_acc[0:2 * P, :]).then_inc(s_out, 16)
            sp.dma_start(y_sample, x_acc[2 * P:NTOK, :]).then_inc(s_out, 16)
            sp.wait_ge(s_out, 32)

        @block.gpsimd
        def _(pool):
            for s in signals:
                s.start(pool)
            pool.memset(ones[:], 1.0)
            pool.memset(eps_t[:], EPS)
            pool.drain()
            pool.affine_select(out=ident[:], in_=ones[:], compare_op=ALU.is_equal, fill=0.0, base=0,
                               pattern=[[-1, P]], channel_multiplier=1).then_inc(s_cst, 1)
            Zq = Z[:]

            def stage_ac(l, br, stage, prep):
                with pool.Fori(0, br.its) as it:
                    pool.wait_ge(pq_done.sem, pq_done.at(l, prep))
                    pool.sem_inc(passed["pool"], 1)
                    pool.wait_ge(pv_mm.sem, pv_mm.at(l, br.hs0 + it * 8 - 1))
                    pool.sem_inc(passed["pool"], 1)
                    qc = pool.snap(it * 4 * HD)
                    kc = pool.snap(it * HD + 512)
                    vc = pool.snap(it * HD + 640)
                    KSv = KS[:].rearrange("p (t c) -> p t c", t=NT)
                    pool.tensor_copy(QS[:].rearrange("p (t c) -> p t c", t=NT), Zq[:, :, bass.ds(qc, 4 * HD)])
                    pool.tensor_copy(KSv[:, :, 0:HD], Zq[:, :, bass.ds(kc, HD)])
                    pool.tensor_copy(KSv[:, :, HD:2 * HD], Zq[:, :, bass.ds(kc, HD)])
                    pool.tensor_copy(VS[:, :, 0:HD], Zq[:, :, bass.ds(vc, HD)])
                    pool.drain().then_inc(staged.sem, 1)
                    norm_p(l, br, it)

            def norm_p(l, br, it):
                nu = len(br.units)
                for u, (h, s, t, last) in enumerate(br.units):
                    pool.wait_ge(p_rec.sem, p_rec.at(l, br.unit0 + it * nu + u))
                    pool.sem_inc(passed["pool"], 1)
                    n = br.nkt(s) * P
                    pool.tensor_scalar(PR[:, u % 3, 0:n], PR[:, u % 3, 0:n], prec[:, u % 4:u % 4 + 1], 1.0,
                                       ALU.mult, ALU.mult).then_inc(p_norm.sem, 1)

            def lo_by_pool(l, e, pos):
                pool.wait_ge(hi_made.sem, hi_made.at(l, NGEMM + e * MPOS + pos))
                pool.tensor_tensor(wlo[:, pos % 2, :], mraw[:, pos % MSLOTS, :], whi[:, pos % 2, :], ALU.subtract)\
                    .then_inc(lo_pool.sem, 1)

            with pool.Fori(0, DEPTH) as l:
                stage_ac(l, BR["A"], 0, PREP_A)
                with pool.Fori(0, BR["B"].its) as it:
                    norm_p(l, BR["B"], it)
                stage_ac(l, BR["C"], 2, PREP_C)
                br = BR["X"]
                with pool.Fori(0, br.its) as it:
                    pool.wait_ge(pq_done.sem, pq_done.at(l, PREP_X))
                    pool.sem_inc(passed["pool"], 1)
                    pool.wait_ge(pv_mm.sem, pv_mm.at(l, br.hs0 + it * 4 - 1))
                    pool.sem_inc(passed["pool"], 1)
                    qc = pool.snap(it * 2 * HD)
                    vc = pool.snap(it * 2 * HD + 256)
                    pool.tensor_copy(QS[:, 0:NT * 128].rearrange("p (t c) -> p t c", t=NT), Zq[:, :, bass.ds(qc, 2 * HD)])
                    pool.tensor_copy(KS[:, 0:MT * 128].rearrange("p (t c) -> p t c", t=MT), mkv[:, :, bass.ds(qc, 2 * HD)])
                    pool.tensor_copy(VS[:, 0:MT, :], mkv[:, :, bass.ds(vc, 2 * HD)])
                    pool.drain().then_inc(staged.sem, 1)
                    norm_p(l, br, it)

                def gather(e):
                    pool.drain()
                    pool.indirect_dma_start(XS[:], None, h_rows[:, :], bass.IndirectOffsetOnAxis(ap=ig[:], axis=0))\
                        .then_inc(xs_in.sem, 16)

                pool.wait_ge(top_ev.sem, top_ev.at(l, 0))
                pool.sem_inc(passed["pool"], 1)
                for i in range(2):
                    pool.wait_ge(h_out[i].sem, h_out[i].at(l, 2))
                    pool.sem_inc(passed["pool"], 1)
                pool.wait_ge(x_out.sem, x_out.at(l, 5))
                pool.sem_inc(passed["pool"], 1)
                pool.tensor_copy(ig[:], idxT[:, 0:1])
                gather(0)
                lo_by_pool(l, 0, 0)

                def expert(e, last):
                    if not last:
                        pool.wait_ge(xs_t.sem, xs_t.at(l, 2 * e + 1))
                        pool.sem_inc(passed["pool"], 1)
                        col = pool.snap(e + 1)
                        pool.tensor_copy(ig[:], idxT[:, bass.ds(col, 1)])
                        gather(e + 1)
                    for pos in range(POOL_EVERY, MPOS, POOL_EVERY):
                        lo_by_pool(l, e, pos)
                    if not last:
                        lo_by_pool(l, e + 1, 0)
                    pool.wait_ge(y_ev.sem, y_ev.at(l, 2 * e + 1))
                    pool.sem_inc(passed["pool"], 1)
                    col = pool.snap(e) if not last else e
                    pool.tensor_copy(isc[:], idxT[:, bass.ds(col, 1)] if not last else idxT[:, e:e + 1])
                    pool.drain()
                    pool.indirect_dma_start(x_acc[:, :], bass.IndirectOffsetOnAxis(ap=isc[:], axis=0), YS[:], None,
                                            compute_op=ALU.add).then_inc(y_out.sem, 16)
                    pool.wait_ge(y_out.sem, y_out.at(l, e))
                    pool.sem_inc(y_done.sem, 1)

                with pool.Fori(0, NE - 1) as e:
                    expert(e, False)
                expert(NE - 1, True)

        @block.scalar
        def _(act):
            def hi_gemm(l, slot, k, used, last_use):
                act.wait_ge(w_in_slot[slot].sem, w_in_slot[slot].at(l, k))
                act.wait_ge(used.sem, used.at(l, last_use))
                act.activation(whi[:, slot, :], wraw[:, slot, :], ACT.Copy).then_inc(hi_made.sem, 1)

            def hi_moe(l, e, pos):
                act.wait_ge(m_in_slot[pos % MSLOTS].sem, m_in_slot[pos % MSLOTS].at(l, 2 * e + pos // MSLOTS))
                act.wait_ge(m_used.sem, m_used.at(l, e * MPOS + pos - 2))
                act.activation(whi[:, pos % 2, :], mraw[:, pos % MSLOTS, :], ACT.Copy).then_inc(hi_made.sem, 1)

            def root(out, n, count):
                act.activation(out, out, ACT.Sqrt, bias=eps_t[:, 0:1], scale=1.0 / count)

            def rows(l, its, i0):
                with act.Fori(0, its) as it:
                    for b in range(2):
                        act.wait_ge(xin_in[b].sem, xin_in[b].at(l, it + i0 // 2))
                        act.activation(nscr[:, b, :], xin[:, b, :], ACT.Square, accum_out=row_ss[:, b:b + 1])
                        act.drain()
                        act.activation(row_rt[:, b:b + 1], row_ss[:, b:b + 1], ACT.Sqrt, bias=eps_t[:, 0:1],
                                       scale=1.0 / D).then_inc(row_root.sem, 1)
                    for b in range(2):
                        act.wait_ge(row_turned.sem, row_turned.at(l, it * 2 + b + i0))
                        act.sem_inc(passed["act"], 1)
                        c = act.snap((it * 2 + b) * P)
                        for h in range(2):
                            ins = act.activation(hT_hi[:, 4 * h:4 * h + 4, bass.ds(c, P)],
                                                 bank[2 * b + h][:].rearrange("p (k n) -> p k n", k=4), ACT.Copy)
                        ins.then_inc(row_hi.sem, 1)

            def z_rows(l, name):
                for n, (j, c, width) in enumerate(Z_CHUNKS[name]):
                    if j != GATE0 - 1:
                        hi_gemm(l, (j + 1) % 2, (j + 1) // 2,
                                *((z_mm, (j - 3) * NT + NT - 1) if j > 2 else (mem_mm, 2 * MT - 1)))
                    for t in range(NT):
                        g = Z_GROUP[name] + n * NT + t
                        act.wait_ge(z_mm.sem, z_mm.at(l, g))
                        act.activation(Z[:, t, c:c + width], bank[g % 4][:, 0:width], ACT.Copy).then_inc(z_ev.sem, 1)
                act.drain()

            def squares(l, parts, k):
                for out, in_ in parts:
                    ins = act.activation(out, in_, ACT.Square)
                ins.then_inc(pq_sq.sem, 1)

            def roots(l, parts, k):
                act.wait_ge(pq_sum.sem, pq_sum.at(l, k))
                for out, count in parts:
                    ins = act.activation(out, out, ACT.Sqrt, bias=eps_t[:, 0:1], scale=1.0 / count)
                ins.then_inc(pq_root.sem, 1)

            def prep_copies(l, k0, parts):
                for i, (dst, rows, cols) in enumerate(parts):
                    act.wait_ge(prep_t.sem, prep_t.at(l, k0 + i))
                    act.activation(dst, bank[7 if i % 2 == 0 else 0][0:rows, 0:cols], ACT.Copy)\
                       .then_inc(prep_ev.sem, 1)

            def attend(l, br, it):
                nu = len(br.units)
                u0 = br.unit0 + it * nu

                def exps(u):
                    h, s, t, last = br.units[u]
                    n = br.nkt(s) * P
                    act.wait_ge(sc_max.sem, sc_max.at(l, u0 + u))
                    if br.name == "C":
                        src = PR[:, u % 3, 0:n]
                        act.activation(esink[:, u % 4:u % 4 + 1], it_sink[:, h:h + 1], ACT.Exp,
                                       bias=nmax[:, u % 4:u % 4 + 1])
                    else:
                        act.wait_ge(p_turn.sem, p_turn.at(l, u0 + u - 3))
                        src = bank[u % 3][:, 0:n]
                    act.activation(PR[:, u % 3, 0:n], src, ACT.Exp, bias=nmax[:, u % 4:u % 4 + 1],
                                   accum_out=psums[:, u % 4:u % 4 + 1]).then_inc(p_exp.sem, 1)

                exps(0)
                exps(1)
                for u, (h, s, t, last) in enumerate(br.units):
                    if u + 2 < nu:
                        exps(u + 2)
                    act.wait_ge(p_turn.sem, p_turn.at(l, u0 + u))
                    t0, _ = SEQS[s]
                    if t == t0:
                        act.wait_ge(pv_mm.sem, pv_mm.at(l, br.hs0 + it * (2 * br.heads) + br.hs(u) - 2))
                    n = br.nkt(s)
                    act.activation(PT[:, br.hs(u) % 2, 0:n, (t - t0) * P:(t - t0 + 1) * P],
                                   bank[3 + u % 2][:, 0:n * P].rearrange("p (k n) -> p k n", k=n), ACT.Copy)\
                       .then_inc(p_ev.sem, 1)

            SQ = PT[:].rearrange("p a b c -> p (a b c)")

            def heads_ac(l, br, prep):
                squares(l, [(SQ[:, 0:NT * 640].rearrange("p (t c) -> p t c", t=NT), Z[:, :, 0:640])], prep)
                roots(l, [(stat[:, 0:60], HD)], prep)
                with act.Fori(0, br.its) as it:
                    prep_copies(l, it * br.nprep + br.prep0,
                                [(QT[:, j, c:c + n], P, n) for j in range(2) for c, n in ((0, 512), (512, 256))]
                                + [(KT[:, 0, c:c + n], P, n) for c, n in ((0, 512), (512, 256))])
                    attend(l, br, it)

            act.wait_ge(s_cst, 1)
            with act.Fori(0, DEPTH) as l:
                hi_gemm(l, 0, 0, m_used, -2)
                rows(l, MT // 2, 0)
                for c in range(2):
                    hi_gemm(l, (c + 1) % 2, (c + 1) // 2,
                            *((m_used, -1) if c == 0 else (mem_mm, MT - 1)))
                    for m in range(MT):
                        g = c * MT + m
                        act.wait_ge(mem_mm.sem, mem_mm.at(l, g))
                        act.activation(mkv[:, m, c * CW:(c + 1) * CW], bank[4 + g % 4][:, 0:CW], ACT.Copy)\
                           .then_inc(mem_ev.sem, 1)
                rows(l, NT // 2, MT)
                z_rows(l, "A")
                heads_ac(l, BR["A"], PREP_A)
                z_rows(l, "B")
                squares(l, [(SQ[:, 0:NT * 640].rearrange("p (t c) -> p t c", t=NT), Z[:, :, 0:640])], PREP_BC)
                roots(l, [(stat[:, 0:6], QR), (stat[:, 6:12], KVR)], PREP_BC)
                prep_copies(l, B_CPREP0, [(cT[:, k, c:c + n], P, n) for k in range(5) for c, n in ((0, 512), (512, 256))])
                br = BR["B"]
                with act.Fori(0, br.its) as it:
                    for t in range(NT):
                        act.wait_ge(bp_mm.sem, bp_mm.at(l, it * NT + t))
                        b = bank[1 + t % 2]
                        kv = b[:, 256:512].rearrange("p (h c) -> p h c", h=2)
                        act.activation(QS[:, t * 2 * BQK:(t + 1) * 2 * BQK], b[:, 0:2 * BQK], ACT.Copy)
                        act.activation(KS[:, t * 2 * BQK:(t + 1) * 2 * BQK].rearrange("p (h c) -> p h c", h=2)[:, :, 0:HD],
                                       kv[:, :, 0:HD], ACT.Copy)
                        act.activation(VS[:, t, :].rearrange("p (h c) -> p h c", h=2), kv[:, :, HD:2 * HD], ACT.Copy)\
                           .then_inc(bp_ev.sem, 1)
                    n = 2 * NT * BQK
                    act.drain()
                    act.wait_ge(krope_in.sem, krope_in.at(l, it))
                    squares(l, [(SQ[:, 0:n], QS[:, 0:n]), (SQ[:, n:2 * n], KS[:, 0:n])], None)
                    roots(l, [(stat[:, 0:24], BQK)], it + PREP_BP)
                    prep_copies(l, it * br.nprep + br.prep0,
                                [(T[0:BQK, h, c:c + n], BQK, n) for T in (QT, KT) for h in range(2)
                                 for c, n in ((0, 512), (512, 256))])
                    attend(l, br, it)
                z_rows(l, "C")
                heads_ac(l, BR["C"], PREP_C)
                z_rows(l, "X")
                squares(l, [(SQ[:, 0:NT * 256].rearrange("p (t c) -> p t c", t=NT), Z[:, :, 0:256]),
                            (SQ[:, NT * 256:(NT + MT) * 256].rearrange("p (t c) -> p t c", t=MT), mkv[:, :, 0:256])], None)
                roots(l, [(stat[:, 0:40], HD)], PREP_X)
                br = BR["X"]
                with act.Fori(0, br.its) as it:
                    prep_copies(l, it * br.nprep + br.prep0,
                                [(QT[:, 0, 0:512], P, 512), (QT[:, 0, 512:768], P, 256),
                                 (KT[:, 0, 0:256], P, 256), (KT[:, 0, 256:512], P, 256)])
                    attend(l, br, it)
                hi_gemm(l, 0, GATE0 // 2, z_mm, 9 * NT - 1)

                def gates(n, last):
                    for b in range(4):
                        if not (last and b == 3):
                            hi_gemm(l, (b + 1) % 2, n * 2 + (GATE0 + b + 1) // 2,
                                    gate_mm, n * 24 + (b * NT - 1))
                        for t in range(NT):
                            g = b * NT + t
                            act.wait_ge(gate_mm.sem, gate_mm.at(l, n * 24 + g))
                            act.wait_ge(gate_mg.sem, gate_mg.at(l, n * 24 + g - 2))
                            act.activation(sgb[:, g % 2, :], bank[g % 2][:, 0:CW], ACT.Sigmoid).then_inc(gate_sg.sem, 1)
                    for h in range(2):
                        for i, (c, w_) in enumerate(((0, 512), (512, 256))):
                            act.wait_ge(mg_t.sem, mg_t.at(l, n * 4 + 2 * h + i))
                            act.sem_inc(passed["act"], 1)
                            k = act.snap(n * 2 + h) if not last else 2 * n + h
                            dst = mT[:, bass.ds(k, 1), c:c + w_] if not last else mT[:, k:k + 1, c:c + w_]
                            act.activation(dst, bank[6 + i][:, 0:w_].unsqueeze(1), ACT.Copy).then_inc(mg_ev.sem, 1)

                with act.Fori(0, 3) as n:
                    gates(n, False)
                gates(3, True)

                def mean_square(t):
                    act.wait_ge(out_ev.sem, out_ev.at(l, 18 + t))
                    act.activation(nscr2[:], X2[:, t, :], ACT.Square, accum_out=row_ss[:, t % 2:t % 2 + 1])
                    act.drain()
                    act.activation(row_rt[:, t % 2:t % 2 + 1], row_ss[:, t % 2:t % 2 + 1], ACT.Sqrt, bias=eps_t[:, 0:1],
                                   scale=1.0 / D).then_inc(r2_root.sem, 1)

                mean_square(0)
                mean_square(1)
                for t in range(NT):
                    act.wait_ge(rl_mm.sem, rl_mm.at(l, t - 1))
                    for h in range(2):
                        act.wait_ge(r2_turn.sem, r2_turn.at(l, 2 * t + h))
                        act.activation(H2T[:, 4 * h:4 * h + 4, :], bank[4 + h][:].rearrange("p (k n) -> p k n", k=4),
                                       ACT.Copy).then_inc(r2_ev.sem, 1)
                    if t + 2 < NT:
                        mean_square(t + 2)
                    act.wait_ge(rl_max.sem, rl_max.at(l, t))
                    act.activation(lg[:, t, :], bank[6][:, 0:NE], ACT.Exp, bias=rst[:, t, 0:1],
                                   accum_out=rst[:, t, 1:2]).then_inc(rl_exp.sem, 1)
                hi_moe(l, 0, 0)

                def part_copies(l, turned, k, b, dst, done):
                    act.wait_ge(turned.sem, turned.at(l, k))
                    act.activation(dst, bank[b][:, 0:4 * CAP].rearrange("p (k n) -> p k n", k=4), ACT.Copy)\
                       .then_inc(done.sem, 1)

                for h in range(2):
                    part_copies(l, xs_t, h, 7, xsT_hi[:, 4 * h:4 * h + 4, :], xs_hi)

                def expert(e, last):
                    for pos in range(MPOS):
                        if pos + 1 < MPOS:
                            hi_moe(l, e, pos + 1)
                        elif not last:
                            hi_moe(l, e + 1, 0)
                        if pos in (1, 5):
                            i = pos // 4
                            act.wait_ge(m_used.sem, m_used.at(l, MPOS * e + 4 * i + 1))
                            act.wait_ge(act_ok.sem, act_ok.at(l, 2 * e + i - 2))
                            act.activation(sg[:, i, :], bank[2 * i][0:CAP, :], ACT.Silu).then_inc(silu_ok.sem, 1)
                        if pos in (5, 8):
                            i = pos // 8
                            part_copies(l, a_t, 2 * e + i, 6, aT_hi[:, 4 * i:4 * i + 4, :], a_hi)
                        if pos in (7, 9) and not last:
                            i = pos // 9
                            part_copies(l, xs_t, 2 * e + 2 + i, 7, xsT_hi[:, 4 * i:4 * i + 4, :], xs_hi)

                with act.Fori(0, NE - 1) as e:
                    expert(e, False)
                expert(NE - 1, True)

        @block.vector
        def _(dve):
            def lo_gemm(l, j, slot):
                dve.wait_ge(hi_made.sem, hi_made.at(l, j))
                dve.tensor_tensor(wlo[:, slot, :], wraw[:, slot, :], whi[:, slot, :], ALU.subtract)\
                   .then_inc(lo_made.sem, 1)

            def lo_moe(l, e, pos):
                dve.wait_ge(hi_made.sem, hi_made.at(l, NGEMM + e * MPOS + pos))
                dve.tensor_tensor(wlo[:, pos % 2, :], mraw[:, pos % MSLOTS, :], whi[:, pos % 2, :], ALU.subtract)\
                   .then_inc(lo_made.sem, 1)

            def rows(l, its, i0, gain):
                with dve.Fori(0, its) as it:
                    for b in range(2):
                        dve.wait_ge(row_root.sem, row_root.at(l, it * 2 + b + i0))
                        dve.reciprocal(row_rt[:, b:b + 1], row_rt[:, b:b + 1])
                        dve.drain()
                        dve.scalar_tensor_tensor(out=xin[:, b, :], in0=xin[:, b, :], scalar=row_rt[:, b:b + 1],
                                                 in1=gain[:], op0=ALU.mult, op1=ALU.mult).then_inc(row_normed.sem, 1)
                    for b in range(2):
                        c = dve.snap((it * 2 + b) * P)
                        dve.wait_ge(row_hi.sem, row_hi.at(l, it * 2 + b + i0))
                        for h in range(2):
                            ins = dve.tensor_tensor(hT_lo[:, 4 * h:4 * h + 4, bass.ds(c, P)],
                                                    bank[2 * b + h][:].rearrange("p (k n) -> p k n", k=4),
                                                    hT_hi[:, 4 * h:4 * h + 4, bass.ds(c, P)], ALU.subtract)
                        ins.then_inc(row_lo.sem, 1)

            def z_rows(l, name):
                for j, c, width in Z_CHUNKS[name]:
                    if j != GATE0 - 1:
                        lo_gemm(l, j + 1, (j + 1) % 2)

            SQ = PT[:].rearrange("p a b c -> p (a b c)")

            def inv_roots(l, k, parts):
                dve.wait_ge(pq_sq.sem, pq_sq.at(l, k))
                for c, n, size, src in parts:
                    ins = dve.tensor_reduce(stat[:, c:c + n], src, AX.X, ALU.add)
                ins.then_inc(pq_sum.sem, 1)
                dve.wait_ge(pq_root.sem, pq_root.at(l, k))
                n = parts[-1][0] + parts[-1][1]
                dve.reciprocal(stat[:, 0:n], stat[:, 0:n])
                dve.drain()

            def by_stat(t, c, tiles, groups, size):
                v = t.rearrange("p t (g d) -> p t g d", g=groups)
                r = stat[:, c:c + tiles * groups].rearrange("p (t g) -> p t g", t=tiles)
                dve.tensor_tensor(v, v, r.unsqueeze(3).to_broadcast([P, tiles, groups, size]), ALU.mult)

            def by_gain(t, gain, tiles, groups, size):
                v = t.rearrange("p t (g d) -> p t g d", g=groups)
                g = gain.unsqueeze(1).unsqueeze(1).to_broadcast([P, tiles, groups, size])
                dve.tensor_tensor(v, v, g, ALU.mult)

            def rope_a():
                for t in range(NT):
                    z = Z[:, t, 0:640]
                    o = t % 2 * 1280
                    own, other = SQ[:, o:o + 640], SQ[:, o + 640:o + 1280]
                    dve.tensor_tensor(own.rearrange("p (g d) -> p g d", g=10), z.rearrange("p (g d) -> p g d", g=10),
                                      cosA[:, t, :].unsqueeze(1).to_broadcast([P, 10, HD]), ALU.mult)
                    zv = z.rearrange("p (g a b d) -> p (g a) b d", g=10, a=2, b=2)
                    ov = other.rearrange("p (g a b d) -> p (g a) b d", g=10, a=2, b=2)
                    sv = sinA[:, t, :].rearrange("p (a b d) -> p a b d", a=2, b=2)
                    for x in range(2):
                        dve.tensor_tensor(ov[:, :, x, :].rearrange("p (g a) d -> p g a d", g=10),
                                          zv[:, :, 1 - x, :].rearrange("p (g a) d -> p g a d", g=10),
                                          sv[:, :, x, :].unsqueeze(1).to_broadcast([P, 10, 2, 16]), ALU.mult)
                    dve.drain()
                    dve.tensor_tensor(z, own, other, ALU.add)

            def rope_b(T, o):
                v = T[:, 0:2 * NT * BQK].rearrange("p (g d) -> p g d", g=2 * NT)[:, :, HD:BQK]
                own = SQ[:, o:o + 2 * NT * ROPE].rearrange("p (g d) -> p g d", g=2 * NT)
                other = SQ[:, o + 384:o + 384 + 2 * NT * ROPE].rearrange("p (g d) -> p g d", g=2 * NT)
                dve.tensor_tensor(own, v, cosB[:], ALU.mult)
                for x in range(2):
                    a, b = slice(x * 16, x * 16 + 16), slice((1 - x) * 16, (1 - x) * 16 + 16)
                    dve.tensor_tensor(other[:, :, a], v[:, :, b], sinB[:, :, a], ALU.mult)
                dve.drain()
                dve.tensor_tensor(v, own, other, ALU.add)

            def heads_ac(l, br, prep, gq, gk, rope):
                inv_roots(l, prep, [(0, 60, HD, SQ[:, 0:3840].rearrange("p (g d) -> p g d", d=HD))])
                by_stat(Z[:, :, 0:640], 0, NT, 10, HD)
                dve.drain()
                by_gain(Z[:, :, 0:512], g_head[:, gq, :], NT, 8, HD)
                by_gain(Z[:, :, 512:640], g_head[:, gk, :], NT, 2, HD)
                dve.drain()
                if rope:
                    rope_a()
                dve.drain().then_inc(pq_done.sem, 1)
                with dve.Fori(0, br.its) as it:
                    attend(l, br, it)

            def attend(l, br, it):
                nu = len(br.units)
                u0 = br.unit0 + it * nu
                if br.name == "C":
                    c = dve.snap(it * 4)
                    dve.tensor_copy(it_slope[:], slopes[:, bass.ds(c, 4)])
                    dve.tensor_copy(it_sink[:], sinks[:, bass.ds(c, 4)])
                    dve.drain()
                    dve.tensor_scalar(it_nsink[:], it_sink[:], -1.0, None, ALU.mult)
                    dve.drain()

                def maxima(u):
                    h, s, t, last = br.units[u]
                    n = br.nkt(s) * P
                    m = slice(u % 4, u % 4 + 1)
                    dve.wait_ge(sc_mm.sem, sc_mm.at(l, u0 + u))
                    if br.name == "C":
                        dve.wait_ge(p_turn.sem, p_turn.at(l, u0 + u - 3))
                        o = (3 - (t - SEQS[s][0])) * P
                        dve.scalar_tensor_tensor(out=PR[:, u % 3, 0:n], in0=ndist[:, o:o + n], scalar=it_slope[:, h:h + 1],
                                                 in1=bank[u % 3][:, 0:n], op0=ALU.mult, op1=ALU.add)
                        dve.drain()
                        dve.tensor_reduce(nraw[:, m], PR[:, u % 3, 0:n], AX.X, ALU.max, negate=True)
                        dve.drain()
                        dve.tensor_tensor(nmax[:, m], nraw[:, m], it_nsink[:, h:h + 1], ALU.min).then_inc(sc_max.sem, 1)
                    else:
                        dve.tensor_reduce(nmax[:, m], bank[u % 3][:, 0:n], AX.X, ALU.max, negate=True)\
                           .then_inc(sc_max.sem, 1)

                def outputs(u):
                    h, s, t, last = br.units[u]
                    n = it * (br.heads // 2) + (br.pair0 + h // 2)
                    dve.wait_ge(pv_mm.sem, pv_mm.at(l, br.hs0 + it * (2 * br.heads) + br.hs(u)))
                    dve.wait_ge(o_out.sem, o_out.at(l, n - 1))
                    t0, nt = SEQS[s]
                    dve.tensor_copy(OS[:, t0 * P:(t0 + nt) * P], bank[5 + s][:, 0:nt * P]).then_inc(o_ev.sem, 1)

                maxima(0)
                maxima(1)
                due = []
                for u, (h, s, t, last) in enumerate(br.units):
                    dve.wait_ge(p_exp.sem, p_exp.at(l, u0 + u))
                    m = slice(u % 4, u % 4 + 1)
                    if br.name == "C":
                        dve.tensor_tensor(psums[:, m], psums[:, m], esink[:, m], ALU.add)
                        dve.drain()
                    dve.reciprocal(prec[:, m], psums[:, m]).then_inc(p_rec.sem, 1)
                    if u + 2 < nu:
                        maxima(u + 2)
                    if last and h % 2:
                        due.append(u)
                    if due and u >= due[0] + 3:
                        outputs(due.pop(0))
                for u in due:
                    outputs(u)

            dve.wait_ge(s_tab, 6 * 16)
            dve.wait_ge(s_cst, 1)
            with dve.Fori(0, DEPTH) as l:
                dve.wait_ge(gains_in.sem, gains_in.at(l, 11))
                for i in (0, 2, 4):
                    dve.tensor_scalar(g_head[:, i, :], g_head[:, i, :], HD ** -0.5, None, ALU.mult)
                dve.tensor_scalar(g_b[:, 0, :], g_b[:, 0, :], BQK ** -0.5, None, ALU.mult)
                lo_gemm(l, 0, 0)
                rows(l, MT // 2, 0, g_mem)
                lo_gemm(l, 1, 1)
                lo_gemm(l, 2, 0)
                rows(l, NT // 2, MT, g_n1)
                z_rows(l, "A")
                heads_ac(l, BR["A"], PREP_A, 0, 1, True)
                z_rows(l, "B")
                inv_roots(l, PREP_BC, [(0, NT, QR, SQ[:, 0:3840].rearrange("p (t c) -> p t c", t=NT)[:, :, 0:QR]),
                                       (NT, NT, KVR, SQ[:, 0:3840].rearrange("p (t c) -> p t c", t=NT)[:, :, QR:QR + KVR])])
                by_stat(Z[:, :, 0:QR], 0, NT, 1, QR)
                by_stat(Z[:, :, QR:QR + KVR], NT, NT, 1, KVR)
                dve.drain()
                by_gain(Z[:, :, 0:QR + KVR], g_bc[:], NT, 1, QR + KVR)
                dve.drain().then_inc(pq_done.sem, 1)
                br = BR["B"]
                with dve.Fori(0, br.its) as it:
                    dve.wait_ge(bp_mm.sem, bp_mm.at(l, it * NT))
                    KSv = KS[:].rearrange("p (t h c) -> p t h c", t=NT, h=2)
                    for h in range(2):
                        dve.tensor_copy(KSv[:, :, h, HD:BQK], Z[:, :, 640:672])
                    dve.drain().then_inc(krope_in.sem, 1)
                    n = 2 * NT * BQK
                    inv_roots(l, it + PREP_BP,
                              [(0, 24, BQK, SQ[:, 0:2 * n].rearrange("p (g d) -> p g d", d=BQK))])
                    for i, T in enumerate((QS, KS)):
                        by_stat(T[:, 0:n].unsqueeze(1), 12 * i, 1, 12, BQK)
                    dve.drain()
                    for i, T in enumerate((QS, KS)):
                        by_gain(T[:, 0:n].unsqueeze(1), g_b[:, i, :], 1, 12, BQK)
                    dve.drain()
                    rope_b(QS, 0)
                    rope_b(KS, 768)
                    dve.drain().then_inc(pq_done.sem, 1)
                    attend(l, br, it)
                z_rows(l, "C")
                heads_ac(l, BR["C"], PREP_C, 2, 3, False)
                z_rows(l, "X")
                inv_roots(l, PREP_X, [(0, 40, HD, SQ[:, 0:40 * HD].rearrange("p (g d) -> p g d", d=HD))])
                by_stat(Z[:, :, 0:256], 0, NT, 4, HD)
                by_stat(mkv[:, :, 0:256], 24, MT, 4, HD)
                dve.drain()
                by_gain(Z[:, :, 0:256], g_head[:, 4, :], NT, 4, HD)
                by_gain(mkv[:, :, 0:256], g_head[:, 5, :], MT, 4, HD)
                dve.drain().then_inc(pq_done.sem, 1)
                with dve.Fori(0, BR["X"].its) as it:
                    attend(l, BR["X"], it)
                lo_gemm(l, GATE0, 0)

                def gates(n, last):
                    for b in range(4):
                        if not (last and b == 3):
                            lo_gemm(l, n * 4 + (GATE0 + b + 1), (b + 1) % 2)
                        for t in range(NT):
                            g = b * NT + t
                            if b == 0 and t == 0:
                                dve.wait_ge(mg_t.sem, mg_t.at(l, n * 4 - 1))
                            dve.wait_ge(gate_sg.sem, gate_sg.at(l, n * 24 + g))
                            prod = bank[2 + g % 2][:, 0:CW]
                            if b == 0:
                                dve.tensor_tensor(mg[:, t, :], sgb[:, g % 2, :], prod, ALU.mult).then_inc(gate_mg.sem, 1)
                            else:
                                dve.tensor_tensor(gpb[:, g % 2, :], sgb[:, g % 2, :], prod, ALU.mult)
                                dve.drain()
                                dve.tensor_tensor(mg[:, t, :], mg[:, t, :], gpb[:, g % 2, :], ALU.add)\
                                   .then_inc(gate_mg.sem, 1)

                with dve.Fori(0, 3) as n:
                    gates(n, False)
                gates(3, True)

                def residual(g):
                    c, t = g // NT, g % NT
                    dve.wait_ge(out_mm.sem, out_mm.at(l, g))
                    x = X2[:, t, c * CW:(c + 1) * CW]
                    dve.tensor_tensor(x, x, bank[g % 4][:, 0:CW], ALU.add).then_inc(out_ev.sem, 1)

                def norm2(t):
                    dve.wait_ge(r2_root.sem, r2_root.at(l, t))
                    dve.reciprocal(row_rt[:, t % 2:t % 2 + 1], row_rt[:, t % 2:t % 2 + 1])
                    dve.drain()
                    dve.wait_ge(r2_turn.sem, r2_turn.at(l, 2 * (t - 2) + 1))
                    if t >= 2:
                        dve.wait_ge(h_out[t % 2].sem, h_out[t % 2].at(l, t // 2 - 1))
                    dve.scalar_tensor_tensor(out=H2[:, t % 2, :], in0=X2[:, t, :], scalar=row_rt[:, t % 2:t % 2 + 1],
                                             in1=g_n2[:], op0=ALU.mult, op1=ALU.mult).then_inc(r2_normed.sem, 1)

                def affinity(t):
                    dve.wait_ge(rl_mm.sem, rl_mm.at(l, t))
                    dve.tensor_reduce(rst[:, t, 0:1], bank[6][:, 0:NE], AX.X, ALU.max, negate=True).then_inc(rl_max.sem, 1)
                    dve.wait_ge(rl_exp.sem, rl_exp.at(l, t))
                    dve.reciprocal(rst[:, t, 2:3], rst[:, t, 1:2])
                    dve.drain()
                    dve.tensor_scalar(lg[:, t, :], lg[:, t, :], rst[:, t, 2:3], None, ALU.mult).then_inc(rl_aff.sem, 1)

                dve.wait_ge(x_in2.sem, x_in2.at(l, 0))
                dve.wait_ge(gn2_in.sem, gn2_in.at(l, 0))
                for g in range(18):
                    residual(g)
                for i in range(NT + 3):
                    if i < NT:
                        residual(18 + i)
                    if 1 <= i <= NT:
                        norm2(i - 1)
                    if i >= 3:
                        affinity(i - 3)
                dve.wait_ge(aff_t.sem, aff_t.at(l, 0))
                dve.tensor_copy(affT[:, 0:256], bank[6][0:NE, 0:256])
                dve.tensor_copy(affT[:, 256:768], bank[7][0:NE, :])
                dve.drain()
                c = 0
                for (t0, nt), cap in zip(SEQS, CAPS):
                    a = affT[:, t0 * P:(t0 + nt) * P]
                    for _ in range(cap // 8):
                        v = val[:, c:c + 8]
                        dve.max(v, a)
                        dve.drain()
                        dve.max_index(idu[:, c:c + 8], v, a)
                        dve.match_replace(a, v, a, -1.0)
                        dve.drain()
                        c += 8
                dve.tensor_copy(idf[:, 0:CAPS[0]], idu[:, 0:CAPS[0]])
                dve.tensor_scalar(idf[:, CAPS[0]:CAP], idu[:, CAPS[0]:CAP], float(SEQS[1][0] * P), None, ALU.add)
                dve.drain().then_inc(top_done.sem, 1)
                dve.wait_ge(top_t.sem, top_t.at(l, 0))
                dve.tensor_copy(valT[:], bank[4][0:CAP, 0:NE])
                dve.tensor_copy(idxT[:], bank[5][0:CAP, 0:NE])
                dve.drain().then_inc(top_ev.sem, 1)

                def low_parts(hi_done, k, b, dst, hi, done):
                    dve.wait_ge(hi_done.sem, hi_done.at(l, k))
                    dve.tensor_tensor(dst, bank[b][:, 0:4 * CAP].rearrange("p (k n) -> p k n", k=4), hi, ALU.subtract)\
                       .then_inc(done.sem, 1)

                for h in range(2):
                    k = slice(4 * h, 4 * h + 4)
                    low_parts(xs_hi, h, 7, xsT_lo[:, k, :], xsT_hi[:, k, :], xs_lo)

                def expert(e, last):
                    for pos in range(MPOS):
                        if (pos + 1) % POOL_EVERY:
                            lo_moe(l, e, pos + 1)
                        if pos in (3, 7):
                            i = pos // 4
                            dve.wait_ge(m_used.sem, m_used.at(l, MPOS * e + 4 * i + 3))
                            dve.wait_ge(silu_ok.sem, silu_ok.at(l, 2 * e + i))
                            dve.tensor_tensor(act_s[:, i * 512:(i + 1) * 512], sg[:, i, :], bank[2 * i + 1][0:CAP, :],
                                              ALU.mult).then_inc(act_ok.sem, 1)
                        if pos in (5, 8):
                            k = slice(pos // 8 * 4, pos // 8 * 4 + 4)
                            low_parts(a_hi, 2 * e + pos // 8, 6, aT_lo[:, k, :], aT_hi[:, k, :], a_lo)
                        if pos in (7, 9) and not last:
                            k = slice(pos // 9 * 4, pos // 9 * 4 + 4)
                            low_parts(xs_hi, 2 * e + 2 + pos // 9, 7, xsT_lo[:, k, :], xsT_hi[:, k, :], xs_lo)
                        if pos in (10, 11):
                            i = pos - 10
                            ex = dve.snap(e) if not last else e
                            dve.wait_ge(y_done.sem, y_done.at(l, e - 1))
                            dve.wait_ge(m_used.sem, m_used.at(l, MPOS * e + pos))
                            gate = valT[:, bass.ds(ex, 1)] if not last else valT[:, ex:ex + 1]
                            dve.tensor_scalar(YS[:, i * 512:(i + 1) * 512], bank[4 + i][0:CAP, :], gate, None, ALU.mult)\
                               .then_inc(y_ev.sem, 1)

                with dve.Fori(0, NE - 1) as e:
                    expert(e, False)
                expert(NE - 1, True)

        @block.tensor
        def _(pe):
            def product3(out, lhs_hi, lhs_lo, rhs_hi, rhs_lo, first, last):
                pe.matmul(out, lhs_hi, rhs_hi, start=first, stop=False)
                pe.matmul(out, lhs_hi, rhs_lo, start=False, stop=False)
                return pe.matmul(out, lhs_lo, rhs_hi, start=False, stop=last)

            def rows(l, its, i0):
                with pe.Fori(0, its) as it:
                    for b in range(2):
                        i = it * 2 + (b + i0)
                        pe.wait_ge(row_normed.sem, row_normed.at(l, i))
                        pe.wait_ge(row_lo.sem, row_lo.at(l, i - 2))
                        for k in range(KD):
                            ins = pe.transpose(bank[2 * b + k // 4][:, k % 4 * P:(k % 4 + 1) * P],
                                               xin[:, b, k * P:(k + 1) * P], ident[:])
                        ins.then_inc(row_turned.sem, 1)

            def group3(out, t, slot, width):
                wh = whi[:, slot, 0:KD * width].rearrange("p (k n) -> p k n", k=KD)
                wl = wlo[:, slot, 0:KD * width].rearrange("p (k n) -> p k n", k=KD)
                c = slice(t * P, (t + 1) * P)
                for k in range(KD):
                    ins = product3(out, hT_hi[:, k, c], hT_lo[:, k, c], wh[:, k, :], wl[:, k, :], k == 0, k == KD - 1)
                return ins

            def z_rows(l, name):
                for n, (j, c, width) in enumerate(Z_CHUNKS[name]):
                    pe.wait_ge(lo_made.sem, lo_made.at(l, j))
                    for t in range(NT):
                        g = Z_GROUP[name] + n * NT + t
                        pe.wait_ge(z_ev.sem, z_ev.at(l, g - 4))
                        ins = group3(bank[g % 4][:, 0:width], t, j % 2, width)
                        ins.then_inc(z_mm.sem, 1)

            def turns(l, k0, parts):
                for i, (rows_, srcs) in enumerate(parts):
                    pe.wait_ge(prep_ev.sem, prep_ev.at(l, k0 + i - 2))
                    for n, src in enumerate(srcs):
                        ins = pe.transpose(bank[7 if i % 2 == 0 else 0][0:rows_, n * P:(n + 1) * P], src, ident[:])
                    ins.then_inc(prep_t.sem, 1)

            def halves(f):
                return [[f(t) for t in range(0, 4)], [f(t) for t in range(4, NT)]]

            def attend(l, br, it):
                nu = len(br.units)
                u0 = br.unit0 + it * nu
                pe.wait_ge(prep_ev.sem, prep_ev.at(l, it * br.nprep + (br.prep0 + br.nprep - 1)))

                def scores(u):
                    h, s, t, last = br.units[u]
                    pe.wait_ge(p_exp.sem, p_exp.at(l, u0 + u - 3))
                    pe.matmul(bank[u % 3][:, 0:br.nkt(s) * P], br.q(QT, h, t), br.k(KT, h, s), start=True, stop=True)\
                      .then_inc(sc_mm.sem, 1)

                def turn(u):
                    h, s, t, last = br.units[u]
                    pe.wait_ge(p_norm.sem, p_norm.at(l, u0 + u))
                    pe.wait_ge(p_ev.sem, p_ev.at(l, u0 + u - 2))
                    for k in range(br.nkt(s)):
                        ins = pe.transpose(bank[3 + u % 2][:, k * P:(k + 1) * P], PR[:, u % 3, k * P:(k + 1) * P], ident[:])
                    ins.then_inc(p_turn.sem, 1)

                def output(u):
                    h, s, t, last = br.units[u]
                    pe.wait_ge(p_ev.sem, p_ev.at(l, u0 + u))
                    n = it * (br.heads // 2) + (br.pair0 + h // 2)
                    if h % 2 == 0:
                        pe.wait_ge(o_ev.sem, o_ev.at(l, 2 * n + s - 2))
                    nq = SEQS[s][1] * P
                    r = h % 2 * HD
                    nk = br.nkt(s)
                    for k in range(nk):
                        ins = pe.matmul(bank[5 + s][r:r + HD, 0:nq], br.v(VS, h, s, k), PT[:, br.hs(u) % 2, k, 0:nq],
                                        start=k == 0, stop=k == nk - 1)
                    ins.then_inc(pv_mm.sem, 1)

                scores(0)
                scores(1)
                due = []
                for u, (h, s, t, last) in enumerate(br.units):
                    if u + 2 < nu:
                        scores(u + 2)
                    turn(u)
                    for v in due:
                        output(v)
                    due = [u] if last else []
                for v in due:
                    output(v)

            def heads_ac(l, br, stage):
                with pe.Fori(0, br.its) as it:
                    pe.wait_ge(staged.sem, staged.at(l, it + stage))
                    Q = QS[:].rearrange("p (t c) -> p t c", t=NT)
                    K = KS[:].rearrange("p (t c) -> p t c", t=NT)
                    turns(l, it * br.nprep + br.prep0,
                          [(P, x) for j in range(2) for x in halves(lambda t: Q[:, t, j * P:(j + 1) * P])]
                          + [(P, x) for x in halves(lambda t: K[:, t, 0:P])])
                    attend(l, br, it)

            pe.wait_ge(s_cst, 1)
            with pe.Fori(0, DEPTH) as l:
                rows(l, MT // 2, 0)
                pe.wait_ge(row_lo.sem, row_lo.at(l, MT - 1))
                for c in range(2):
                    pe.wait_ge(lo_made.sem, lo_made.at(l, c))
                    for m in range(MT):
                        g = c * MT + m
                        pe.wait_ge(mem_ev.sem, mem_ev.at(l, g - 4))
                        group3(bank[4 + g % 4][:, 0:CW], m, c, CW).then_inc(mem_mm.sem, 1)
                rows(l, NT // 2, MT)
                pe.wait_ge(row_lo.sem, row_lo.at(l, MT + NT - 1))
                z_rows(l, "A")
                heads_ac(l, BR["A"], 0)
                z_rows(l, "B")
                pe.wait_ge(pq_done.sem, pq_done.at(l, PREP_BC))
                turns(l, B_CPREP0, [(P, x) for k in range(5) for x in halves(lambda t: Z[:, t, k * P:(k + 1) * P])])
                pe.wait_ge(prep_ev.sem, prep_ev.at(l, B_CPREP0 + 9))
                pe.sem_inc(passed["pe"], 1)
                br = BR["B"]
                with pe.Fori(0, br.its) as it:
                    pe.wait_ge(bw_in[0].sem, bw_in[0].at(l, it))
                    pe.wait_ge(bw_in[1].sem, bw_in[1].at(l, it))
                    for t in range(NT):
                        b = bank[1 + t % 2]
                        pe.wait_ge(bp_ev.sem, bp_ev.at(l, it * NT + (t - 2)))
                        c = slice(t * P, (t + 1) * P)
                        for k in range(3):
                            pe.matmul(b[:, 0:2 * BQK], cT[:, k, c], wqp[:, k, :], start=k == 0, stop=k == 2)
                        for k in range(2):
                            ins = pe.matmul(b[:, 256:512], cT[:, 3 + k, c], wkvp[:, k, :], start=k == 0, stop=k == 1)
                        ins.then_inc(bp_mm.sem, 1)
                    pe.wait_ge(pq_done.sem, pq_done.at(l, it + PREP_BP))

                    def head(T, h):
                        return halves(lambda t: T[:, t * 2 * BQK + h * BQK:t * 2 * BQK + (h + 1) * BQK])

                    turns(l, it * br.nprep + br.prep0, [(BQK, x) for T in (QS, KS) for h in range(2) for x in head(T, h)])
                    attend(l, br, it)
                z_rows(l, "C")
                heads_ac(l, BR["C"], 2)
                z_rows(l, "X")
                br = BR["X"]
                with pe.Fori(0, br.its) as it:
                    pe.wait_ge(staged.sem, staged.at(l, it + 4))
                    qx = [QS[:, t * P:(t + 1) * P] for t in range(NT)]
                    kx = [KS[:, t * P:(t + 1) * P] for t in range(MT)]
                    turns(l, it * br.nprep + br.prep0, [(P, qx[0:4]), (P, qx[4:6]), (P, kx[0:2]), (P, kx[2:4])])
                    attend(l, br, it)
                pe.wait_ge(o_in.sem, o_in.at(l, 0))
                pe.sem_inc(passed["pe"], 1)

                def gates(n):
                    for b in range(4):
                        pe.wait_ge(lo_made.sem, lo_made.at(l, n * 4 + (GATE0 + b)))
                        if b % 2 == 0:
                            pe.wait_ge(d_in[b // 2].sem, d_in[b // 2].at(l, n))
                        nk = 2 if b == 3 else 4
                        for t in range(NT):
                            g = b * NT + t
                            pe.wait_ge(gate_mg.sem, gate_mg.at(l, n * 24 + (g - 2)))
                            group3(bank[g % 2][:, 0:CW], t, b % 2, CW)
                            for k in range(nk):
                                kk = b % 2 * 4 + k
                                ins = pe.matmul(bank[2 + g % 2][:, 0:CW], oT[:, 4 * b + k, t * P:(t + 1) * P],
                                                wdir[:, b // 2, kk * CW:(kk + 1) * CW], start=k == 0, stop=k == nk - 1)
                            ins.then_inc(gate_mm.sem, 1)
                    pe.wait_ge(gate_mg.sem, gate_mg.at(l, n * 24 + 23))
                    for h in range(2):
                        for i, ts in enumerate((range(0, 4), range(4, NT))):
                            pe.wait_ge(mg_ev.sem, mg_ev.at(l, n * 4 + (2 * h + i - 2)))
                            for m, t in enumerate(ts):
                                ins = pe.transpose(bank[6 + i][:, m * P:(m + 1) * P], mg[:, t, h * P:(h + 1) * P], ident[:])
                            ins.then_inc(mg_t.sem, 1)

                with pe.Fori(0, 4) as n:
                    gates(n)
                pe.wait_ge(mg_ev.sem, mg_ev.at(l, 15))

                def project(g):
                    c, t = g // NT, g % NT
                    if t == 0:
                        pe.wait_ge(d_in[c % 2].sem, d_in[c % 2].at(l, 4 + c // 2))
                    pe.wait_ge(out_ev.sem, out_ev.at(l, g - 4))
                    for k in range(KD):
                        ins = pe.matmul(bank[g % 4][:, 0:CW], mT[:, k, t * P:(t + 1) * P],
                                        wdir[:, c % 2, k * CW:(k + 1) * CW], start=k == 0, stop=k == KD - 1)
                    ins.then_inc(out_mm.sem, 1)

                def turn_h(t):
                    pe.wait_ge(r2_normed.sem, r2_normed.at(l, t))
                    for h in range(2):
                        pe.wait_ge(r2_ev.sem, r2_ev.at(l, 2 * (t - 1) + h))
                        for k in range(4):
                            kk = 4 * h + k
                            ins = pe.transpose(bank[4 + h][:, k * P:(k + 1) * P], H2[:, t % 2, kk * P:(kk + 1) * P], ident[:])
                        ins.then_inc(r2_turn.sem, 1)

                def route(t):
                    pe.wait_ge(r2_ev.sem, r2_ev.at(l, 2 * t + 1))
                    pe.wait_ge(rl_exp.sem, rl_exp.at(l, t - 1))
                    for k in range(KD):
                        ins = pe.matmul(bank[6][:, 0:NE], H2T[:, k, :], wr[:, k, :], start=k == 0, stop=k == KD - 1)
                    ins.then_inc(rl_mm.sem, 1)

                pe.wait_ge(g2_in.sem, g2_in.at(l, 1))
                for g in range(18):
                    project(g)
                for i in range(NT + 3):
                    if i < NT:
                        project(18 + i)
                    if i >= 3:
                        route(i - 3)
                    if 2 <= i < NT + 2:
                        turn_h(i - 2)
                pe.wait_ge(rl_aff.sem, rl_aff.at(l, NT - 1))
                pe.sem_inc(passed["pe"], 1)
                for t in range(NT):
                    b, c = (bank[6], t) if t < 2 else (bank[7], t - 2)
                    ins = pe.transpose(b[0:NE, c * P:(c + 1) * P], lg[:, t, :], ident[:])
                ins.then_inc(aff_t.sem, 1)
                pe.wait_ge(top_done.sem, top_done.at(l, 0))
                pe.sem_inc(passed["pe"], 1)
                pe.transpose(bank[4][0:CAP, 0:NE], val[:], ident[0:NE, 0:NE])
                pe.transpose(bank[5][0:CAP, 0:NE], idf[:], ident[0:NE, 0:NE]).then_inc(top_t.sem, 1)

                def turn_part(src, h, b, done):
                    for k in range(4):
                        kk = 4 * h + k
                        ins = pe.transpose(bank[b][:, k * CAP:(k + 1) * CAP], src[:, kk * P:(kk + 1) * P], ident[0:CAP, 0:CAP])
                    ins.then_inc(done.sem, 1)

                def turn_xs(e, h):
                    pe.wait_ge(xs_in.sem, xs_in.at(l, e))
                    pe.wait_ge(xs_lo.sem, xs_lo.at(l, 2 * e + (h - 1)))
                    turn_part(XS, h, 7, xs_t)

                turn_xs(0, 0)
                turn_xs(0, 1)

                def expert(e, last):
                    pe.wait_ge(xs_lo.sem, xs_lo.at(l, 2 * e + 1))
                    for pos in range(MPOS):
                        if pos % POOL_EVERY == 0:
                            pe.wait_ge(lo_pool.sem, lo_pool.at(l, e * (MPOS // POOL_EVERY) + pos // POOL_EVERY))
                        else:
                            pe.wait_ge(lo_made.sem, lo_made.at(l, m_lo_index(e, pos)))
                        wh = whi[:, pos % 2, :].rearrange("p (k n) -> p k n", k=4)
                        wl = wlo[:, pos % 2, :].rearrange("p (k n) -> p k n", k=4)
                        if pos < 8:
                            if pos % 4 == 0:
                                pe.wait_ge(act_ok.sem, act_ok.at(l, 2 * e + (pos // 4 - 2)))
                            out, hi, lo, half = bank[pos // 2][0:CAP, :], xsT_hi, xsT_lo, pos % 2
                        else:
                            i, half = (pos - 8) % 2, (pos - 8) // 2
                            if i == 0:
                                pe.wait_ge(a_lo.sem, a_lo.at(l, 2 * e + half))
                            if half == 0:
                                pe.wait_ge(y_ev.sem, y_ev.at(l, 2 * e + (i - 2)))
                            out, hi, lo = bank[4 + i][0:CAP, :], aT_hi, aT_lo
                        for k in range(4):
                            kk = half * 4 + k
                            ins = product3(out, hi[:, kk, :], lo[:, kk, :], wh[:, k, :], wl[:, k, :],
                                           half == 0 and k == 0, half == 1 and k == 3)
                        ins.then_inc(m_used.sem, 1)
                        if pos in (5, 8):
                            i = pos // 8
                            pe.wait_ge(act_ok.sem, act_ok.at(l, 2 * e + i))
                            pe.wait_ge(a_lo.sem, a_lo.at(l, 2 * e + (i - 1)))
                            turn_part(act_s, i, 6, a_t)
                        if pos in (7, 9) and not last:
                            turn_xs(e + 1, pos // 9)

                with pe.Fori(0, NE - 1) as e:
                    expert(e, False)
                expert(NE - 1, True)


_W = ['w_in', 'b_w_q_b', 'b_w_kv_b', 'w_mem_kv', 'w_branch', 'w_out', 'w_router', 'w_gate_up', 'w_down']
_G = ['norm1_g', 'a_q_norm', 'a_k_norm', 'b_q_a_norm', 'b_kv_a_norm', 'b_q_norm', 'b_k_norm', 'c_q_norm', 'c_k_norm',
      'c_sink', 'x_q_norm', 'x_k_norm', 'mem_norm_g', 'norm2_g']


def shape_tables():
    import numpy as np
    theta, grid_w = np.float32(10000.0), 64

    def angles(pos, dim):
        inv = np.power(theta, -np.arange(0, dim, 2, dtype=np.float32) / np.float32(dim)).astype(np.float32)
        return pos.astype(np.float32)[:, None] * inv[None, :]

    def rotary(ang):
        c, s = np.cos(ang).astype(np.float32), np.sin(ang).astype(np.float32)
        return np.concatenate([c, c], 1), np.concatenate([-s, s], 1)

    pos = np.concatenate([np.arange(n * P) for _, n in SEQS])
    (cr, sr), (cc, sc) = rotary(angles(pos // grid_w, HD // 2)), rotary(angles(pos % grid_w, HD // 2))
    cb, sb_ = rotary(angles(pos, ROPE))

    def tiles(a):
        return np.ascontiguousarray(a.reshape(NT, P, -1).transpose(1, 0, 2))

    cb, sb_ = (np.repeat(tiles(a), 2, axis=1) for a in (cb, sb_))
    dist = np.abs(np.arange(7 * P)[None, :] - 3 * P - np.arange(P)[:, None]).astype(np.float32)
    slopes = np.power(np.float32(2.0), -np.arange(1, 9, dtype=np.float32))
    return {"cosA": tiles(np.concatenate([cr, cc], 1)), "sinA": tiles(np.concatenate([sr, sc], 1)),
            "cosB": np.ascontiguousarray(cb), "sinB": np.ascontiguousarray(sb_),
            "ndist": np.where(dist <= 128, -dist, np.float32(-1e30)).astype(np.float32),
            "slopes": np.ascontiguousarray(np.broadcast_to(slopes, (P, 8)))}


def kernel(**inputs):
    import numpy as _np
    import concourse.bacc as _bacc
    from concourse import mybir as _mybir
    from concourse.bass_utils import run_bass_kernel_spmd as _run

    nc = _bacc.Bacc("TRN2", target_bir_lowering=False, num_devices=1, dynamic_dma_scratch_size=4096)
    arrays = {}

    def give(name, a):
        a = _np.ascontiguousarray(a)
        arrays[f"in_{name}_dram"] = a
        return nc.dram_tensor(f"in_{name}_dram", a.shape, _mybir.dt.from_np(a.dtype), kind="ExternalInput").ap()

    x = give("x", _np.concatenate([inputs["x_prompt"][0], inputs["x_sample"][0]], 0))
    mem = give("mem", _np.concatenate([inputs["mem_prompt"][0], inputs["mem_sample"][0]], 0))
    w = {n: give(n, inputs[n]) for n in _W}
    for n in ("w_gate_up", "w_down"):
        w[n] = w[n].rearrange("l e d f -> (l e) d f")
    g = {n: give(n, inputs[n]) for n in _G}
    tables = {n: give(n, a) for n, a in shape_tables().items()}
    outs = [nc.dram_tensor(f"out_{i}_dram", (1, n * P, D), _mybir.dt.float32, kind="ExternalOutput").ap()
            for i, (_, n) in enumerate(SEQS)]
    build(nc, x, mem, w, g, tables, outs[0][0], outs[1][0])
    r = _run(nc, [arrays], core_ids=[0])
    return tuple(r.results[0][f"out_{i}_dram"] for i in range(2))
```

```python
from contextlib import ExitStack

import concourse.bass as bass
from concourse import mybir

F32 = mybir.dt.float32
F32R = mybir.dt.float32r
U32 = mybir.dt.uint32
ALU = mybir.AluOpType
ACT = mybir.ActivationFunctionType
AX = mybir.AxisListType

P = 128
DEPTH = 2
D = 1024
KD = D // P
SEQS = [(0, 2), (2, 4)]
NT = 6
NTOK = NT * P
MT = 4
HD = 64
QR, KVR, ROPE = 384, 256, 32
BQK = HD + ROPE
EPS = 1e-6
NE = 16
CAPS = [32, 64]
CAP = sum(CAPS)
DE = 1024

IN_A, IN_B, IN_C, IN_X, IN_G = 0, 768, 1440, 2208, 2464

CW = 256
SLOT = KD * CW
Z_CHUNKS = {
    "A": [(2, 0, 256), (3, 256, 256), (4, 512, 256)],
    "B": [(5, 0, 256), (6, 256, 256), (7, 512, 160)],
}
Z_BASE = {"A": IN_A, "B": IN_B}
CX0 = 8
GATE0 = 12
NGEMM = 28
MPOS = 12
NCHUNK = NGEMM + NE * MPOS
MSLOTS = 6
WSLOTS = 4
AHEAD = 3
POOL_EVERY = 3
LO_PER_E = MPOS - MPOS // POOL_EVERY

LEAD = 16


class Signal:

    def __init__(self, sem, n, unit=1, lead=LEAD):
        self.sem, self.n, self.unit, self.lead = sem, n, unit, lead

    def start(self, eng):
        if self.lead:
            eng.sem_inc(self.sem, self.lead * self.unit)

    def at(self, layer, k):
        return (layer * self.n + k + 1 + self.lead) * self.unit


class Branch:
    def __init__(self, name, its, heads, rows, unit0, hs0, pair0, prep0, nprep):
        self.name, self.its, self.heads, self.rows = name, its, heads, rows
        self.unit0, self.hs0, self.pair0, self.prep0, self.nprep = unit0, hs0, pair0, prep0, nprep
        self.units = []
        for pair in range(heads // 2):
            for s, (t0, n) in enumerate(SEQS):
                for h in (2 * pair, 2 * pair + 1):
                    for t in range(t0, t0 + n):
                        self.units.append((h, s, t, t == t0 + n - 1))

    def hs(self, u):
        return sum(last for *_, last in self.units[:u])

    def last_prep(self, it):
        return self.prep0 + (it + 1) * self.nprep - 1

    def nkt(self, s):
        return 2 if self.name == "X" else SEQS[s][1]

    def window(self, u):
        h, s, t, last = self.units[u]
        if self.name != "C":
            return 0, self.nkt(s)
        t -= SEQS[s][0]
        k0 = max(0, t - 1)
        return k0, min(self.nkt(s), t + 2) - k0

    def key_tile(self, s):
        return 2 * s if self.name == "X" else SEQS[s][0]

    def q(self, QT, h, t):
        c = slice(t * P, (t + 1) * P)
        if self.name == "B":
            return QT[0:BQK, h, c]
        return QT[(h % 2) * HD:(h % 2 + 1) * HD, h // 2, c]

    def k(self, KT, u):
        h, s, t, last = self.units[u]
        k0, nk = self.window(u)
        c = slice((self.key_tile(s) + k0) * P, (self.key_tile(s) + k0 + nk) * P)
        if self.name == "B":
            return KT[0:BQK, h, c]
        return KT[(h % 2) * HD:(h % 2 + 1) * HD, h // 2 if self.name == "X" else 0, c]


BR = {
    "A": Branch("A", 2, 4, HD, 0, 0, 0, 0, 6),
    "B": Branch("B", 4, 2, BQK, 48, 16, 4, 22, 8),
    "C": Branch("C", 2, 4, HD, 96, 32, 8, 54, 6),
    "X": Branch("X", 1, 4, HD, 144, 48, 12, 66, 6),
}
B_CPREP0 = 12
PREP_A, PREP_BP, PREP_C, PREP_X, NPREP = 0, 1, 5, 6, 7


def build(nc, x_in, mem_in, w, gains, tables, y_prompt, y_sample):
    ctx = ExitStack()
    with ctx:
        def sb(name, shape, dt=F32):
            return ctx.enter_context(nc.sbuf_tensor(name, shape, dt))

        signals = []

        def sig(name, n, unit=1, lead=LEAD):
            s = Signal(ctx.enter_context(nc.semaphore(name)), n, unit, lead)
            signals.append(s)
            return s

        def dma_sig(name, n):
            return sig(name, n, 16)

        x_acc = nc.dram_tensor("x_acc", [NTOK, D], F32)
        h_rows = nc.dram_tensor("h_rows", [NTOK, D], F32)
        o_rows = nc.dram_tensor("o_rows", [12 * P, NTOK], F32)

        wraw = sb("wraw", [P, 2, SLOT])
        whi = sb("whi", [P, 2, SLOT], F32R)
        wlo = sb("wlo", [P, 2, SLOT], F32R)
        mkv = sb("mkv", [P, MT, 2 * 4 * HD])
        ident = sb("ident", [P, P])
        ones = sb("ones", [P, P])
        eps_t = sb("eps_t", [P, 1])
        cosB = sb("cosB", [P, 2 * NT, ROPE])
        sinB = sb("sinB", [P, 2 * NT, ROPE])
        ndist = sb("ndist", [P, 7 * P])
        slopes = sb("slopes", [P, 8])
        sinks = sb("sinks", [P, 8])
        g_head = sb("g_head", [P, 6, HD])
        g_b = sb("g_b", [P, 2, BQK])
        g_bc = sb("g_bc", [P, QR + KVR])
        stat = sb("stat", [P, 64])
        row_ss = sb("row_ss", [P, MT + NT])
        row_rt = sb("row_rt", [P, MT + NT])
        nmax = sb("nmax", [P, 4])
        nraw = sb("nraw", [P, 4])
        psums = sb("psums", [P, 4])
        esink = sb("esink", [P, 4])
        prec = sb("prec", [P, 4])
        it_slope = sb("it_slope", [P, 4])
        it_sink = sb("it_sink", [P, 4])
        it_nsink = sb("it_nsink", [P, 4])

        wr = sb("wr", [P, KD, NE])
        lg = sb("lg", [P, NT, NE])
        rst = sb("rst", [P, NT, 4])
        val = sb("val", [NE, CAP])
        idu = sb("idu", [NE, CAP], U32)
        idf = sb("idf", [NE, CAP])
        valT = sb("valT", [CAP, NE])
        idxT = sb("idxT", [CAP, NE], U32)
        ig = sb("ig", [CAP, 1], U32)
        isc = sb("isc", [CAP, 1], U32)

        def region(name, size):
            slab = sb(name, [P, size // 4])
            start = nc.sbuf_base - size

            def plan():
                at = [0]

                def take(name, shape, dt=F32):
                    n = 4
                    for m in shape[1:]:
                        n *= m
                    t = nc.alloc_sbuf_tensor_at(name, shape, dt, offset=start + at[0])
                    at[0] += n
                    assert at[0] <= size, (name, at[0], size)
                    return t
                return take
            return plan

        rows_region = region("rows_region", 2 * KD * NTOK * 4)
        arena = region("arena", 93952)
        small = region("small", 4352)

        take = small()
        wqp = take("wqp", [P, 3, 2 * BQK])
        wkvp = take("wkvp", [P, 2, 4 * HD])
        take = small()
        sgb = take("sgb", [P, 2, CW])
        gpb = take("gpb", [P, 2, CW])

        take = rows_region()
        hT_hi = take("hT_hi", [P, KD, NTOK], F32R)
        hT_lo = take("hT_lo", [P, KD, NTOK], F32R)
        take = rows_region()
        X2 = take("X2", [P, NT, D])
        g_n2 = take("g_n2", [P, D])
        H2 = take("H2", [P, 2, D])
        nscr2 = take("nscr2", [P, D])
        H2T = take("H2T", [P, KD, P])
        affT = take("affT", [NE, NTOK])
        take = rows_region()
        XS = take("XS", [CAP, D])
        xsT_hi = take("xsT_hi", [P, KD, CAP], F32R)
        xsT_lo = take("xsT_lo", [P, KD, CAP], F32R)
        sg = take("sg", [CAP, 2, 512])
        act_s = take("act_s", [CAP, DE])
        aT_hi = take("aT_hi", [P, KD, CAP], F32R)
        aT_lo = take("aT_lo", [P, KD, CAP], F32R)
        YS = take("YS", [CAP, D])
        take = arena()
        xin = take("xin", [P, MT + NT, D])
        g_mem = take("g_mem", [P, D])
        g_n1 = take("g_n1", [P, D])
        nscr = take("nscr", [P, D])
        take = arena()
        Z = take("Z", [P, 4, NT, 256])
        ZB = take("ZB", [P, NT, QR + KVR])
        krope = take("krope", [P, NT, ROPE])
        cT = take("cT", [P, 5, NTOK])
        OS = take("OS", [P, NTOK])
        QT = take("QT", [P, 2, NTOK])
        KT = take("KT", [P, 2, NTOK])
        PR = take("PR", [P, 3, 512])
        PT = take("PT", [P, 2, 4, 512])
        take = arena()
        take("before_QS", [P, 4, NT, 256])
        QS = take("QS", [P, NT * 2 * BQK])
        KS = take("KS", [P, NT * 2 * BQK])
        VS = take("VS", [P, NT, 2 * HD])
        take = arena()
        take("before_KC", [P, 4, NT, 256])
        KC = take("KC", [P, NT, 256])
        take = arena()
        take("before_cosA", [P, (4 * 256 + QR + KVR + ROPE + 5 * P) * NT])
        cosA = take("cosA", [P, NT, HD])
        sinA = take("sinA", [P, NT, HD])
        take = arena()
        oT = take("oT", [P, 14, NTOK])
        mg = take("mg", [P, NT, CW])
        wdir = take("wdir", [P, 2, SLOT])
        mT = take("mT", [P, KD, NTOK])
        take = arena()
        mraw = take("mraw", [P, MSLOTS, SLOT])
        take("before_whi_more", [P, (93952 // 4) - (MSLOTS + 2 * (WSLOTS - 2)) * SLOT])
        whi_more = take("whi_more", [P, WSLOTS - 2, SLOT], F32R)
        wlo_more = take("wlo_more", [P, WSLOTS - 2, SLOT], F32R)

        def m_hi(pos):
            i = pos % WSLOTS
            return whi[:, i, :] if i < 2 else whi_more[:, i - 2, :]

        def m_lo(pos):
            i = pos % WSLOTS
            return wlo[:, i, :] if i < 2 else wlo_more[:, i - 2, :]

        bank = [ctx.enter_context(nc.psum_tensor(f"bank{i}", [P, 512], F32)) for i in range(8)]

        def row_bank(i, h):
            return bank[(0 if i < MT else 4) + 2 * (i % 2) + h]

        prep_banks = [bank[i] for i in (7, 0, 1, 2)]
        score_banks = [bank[i] for i in (0, 1, 2, 7)]

        s_x0 = ctx.enter_context(nc.semaphore("x0_stored"))
        s_tab = ctx.enter_context(nc.semaphore("tables_loaded"))
        s_cst = ctx.enter_context(nc.semaphore("consts_made"))
        passed = {e: ctx.enter_context(nc.semaphore(f"passed_{e}")) for e in ("act", "pool", "pe", "dve", "sp")}
        s_out = ctx.enter_context(nc.semaphore("outputs_stored"))
        gains_in = dma_sig("gains_in", 12)
        krope_in = sig("krope_in", 4)
        g2_in = dma_sig("g2_in", 2)
        gn2_in = dma_sig("gn2_in", 1)
        w_in_slot = [dma_sig(f"w_in_slot{i}", NGEMM // 2) for i in range(2)]
        m_in_slot = [dma_sig(f"m_in_slot{i}", NE * MPOS // MSLOTS) for i in range(MSLOTS)]
        hi_made = sig("hi_made", NCHUNK)
        lo_made = sig("lo_made", NGEMM + LO_PER_E * NE)
        lo_pool = sig("lo_pool", (MPOS - LO_PER_E) * NE)
        xin_in = [dma_sig(f"xin_in{i}", 1) for i in range(3)]
        row_root = sig("row_root", 2)
        row_normed = sig("row_normed", 10)
        row_turned = sig("row_turned", 10)
        row_hi = sig("row_hi", 10)
        row_lo = sig("row_lo", 10)
        mem_mm = sig("mem_mm", 8)
        mem_ev = sig("mem_ev", 8)
        z_mm = sig("z_mm", 60)
        z_ev = sig("z_ev", 60)
        pq_sq = sig("pq_sq", NPREP)
        tabA_in = dma_sig("tabA_in", 2)
        pq_sum = sig("pq_sum", NPREP)
        pq_root = sig("pq_root", NPREP)
        bc_root = sig("bc_root", 1)
        bc_done = sig("bc_done", 1)
        pq_done = sig("pq_done", NPREP)
        prep_t = sig("prep_t", 72)
        prep_ev = sig("prep_ev", 72)
        bw_in = [dma_sig(f"bw_in{i}", 4) for i in range(2)]
        bp_mm = sig("bp_mm", 24)
        bp_ev = sig("bp_ev", 24)
        sc_mm = sig("sc_mm", 168)
        sc_max = sig("sc_max", 168)
        p_exp = sig("p_exp", 168)
        p_rec = sig("p_rec", 168)
        p_norm = sig("p_norm", 168)
        p_turn = sig("p_turn", 168)
        p_ev = sig("p_ev", 168)
        pv_mm = sig("pv_mm", 56)
        o_ev = sig("o_ev", 28)
        o_out = dma_sig("o_out", 12)
        o_in = dma_sig("o_in", 1)
        d_in = [dma_sig(f"d_in{i}", 6) for i in range(2)]
        gate_mm = sig("gate_mm", 96)
        gate_sg = sig("gate_sg", 96)
        gate_mg = sig("gate_mg", 96)
        mg_t = sig("mg_t", 16)
        mg_ev = sig("mg_ev", 16)
        x_in2 = dma_sig("x_in2", 1)
        out_mm = sig("out_mm", 24)
        out_ev = sig("out_ev", 24)
        r2_root = sig("r2_root", 6)
        r2_normed = sig("r2_normed", 6)
        x_out = dma_sig("x_out", 6)
        h_out = [dma_sig(f"h_out{i}", 3) for i in range(2)]
        r2_turn = sig("r2_turn", 12)
        r2_ev = sig("r2_ev", 12)
        rl_mm = sig("rl_mm", 6)
        rl_max = sig("rl_max", 6)
        rl_exp = sig("rl_exp", 6)
        rl_aff = sig("rl_aff", 6)
        aff_t = sig("aff_t", 1)
        top_done = sig("top_done", 1)
        top_t = sig("top_t", 1)
        top_ev = sig("top_ev", 1)
        ig_ok = sig("ig_ok", NE)
        isc_ok = sig("isc_ok", NE)
        xs_in = sig("xs_in", NE, 16, 0)
        xs_t = sig("xs_t", 2 * NE)
        xs_hi = sig("xs_hi", 2 * NE)
        xs_lo = sig("xs_lo", 2 * NE)
        m_used = sig("m_used", MPOS * NE)
        silu_ok = sig("silu_ok", 2 * NE)
        act_ok = sig("act_ok", 2 * NE)
        a_t = sig("a_t", 2 * NE)
        a_hi = sig("a_hi", 2 * NE)
        a_lo = sig("a_lo", 2 * NE)
        y_ev = sig("y_ev", 2 * NE)
        y_out = sig("y_out", NE, 16, 0)
        y_done = sig("y_done", NE)

        def m_lo_index(e, pos):
            return NGEMM + e * LO_PER_E + pos - pos // POOL_EVERY - 1

        zq = Z[:, 0:2, :, :].rearrange("p c t n -> p (c t) n")
        zk = Z[:, 2, :, 0:2 * HD]
        k_twice = {"A": Z[:, 3, :, :].rearrange("p t (h c) -> p (t h) c", h=2),
                   "C": KC[:].rearrange("p t (h c) -> p (t h) c", h=2)}
        SQ = PT[:].rearrange("p a b c -> p (a b c)")
        sq_q = SQ[:, 0:12 * 256].rearrange("p (r n) -> p r n", r=12)
        sq_k = SQ[:, 12 * 256:12 * 256 + NT * 2 * HD].rearrange("p (t n) -> p t n", t=NT)

        def v_of(br, h, s, kt, it):
            t = br.key_tile(s) + kt
            if br.name == "B":
                return VS[:, t, h * HD:(h + 1) * HD]
            if br.name == "X":
                return mkv[:, t, (4 + h) * HD:(5 + h) * HD]
            return Z[:, 2, t, (2 + it) * HD:(3 + it) * HD]

        def kpn(ap):
            return ap.rearrange("o (k p) n -> (o p) k n", p=P)

        def lay(t, l):
            return t[bass.ds(l, 1)]

        block = ctx.enter_context(nc.Block())

        @block.sync
        def _(sp):
            def load_w(l, j, src, width, rows=KD):
                k = j - 2
                sp.wait_ge(lo_made.sem, lo_made.at(l, k))
                sp.dma_start(wraw[:, j % 2, 0:rows * width].rearrange("p (k n) -> p k n", n=width), src)\
                  .then_inc(w_in_slot[j % 2].sem, 16)

            def load_z(l, name, n):
                j, c, width = Z_CHUNKS[name][n]
                c += Z_BASE[name]
                load_w(l, j, kpn(lay(w["w_in"], l)[:, :, c:c + width]), width)

            def store_pairs(l, br, it):
                for pr in range(br.heads // 2):
                    n = it * (br.heads // 2) + pr + br.pair0
                    row = sp.snap(n * P) if not isinstance(n, int) else n * P
                    sp.wait_ge(o_ev.sem, o_ev.at(l, 2 * n + 1))
                    sp.dma_start(o_rows[bass.ds(row, P), :], OS[:]).then_inc(o_out.sem, 16)

            with sp.Fori(0, DEPTH) as l:
                sp.wait_ge(lo_made.sem, lo_made.at(l, -1))
                sp.wait_ge(y_done.sem, y_done.at(l, -1))
                def load_gain(t, name):
                    sp.dma_start(t, gains[name][bass.ds(l, 1), :].to_broadcast([P, t.shape[-1]]))\
                      .then_inc(gains_in.sem, 16)

                for h in range(2):
                    sp.dma_start(xin[:, 2 * h:2 * h + 2, :],
                                 mem_in[2 * h * P:2 * (h + 1) * P, :].rearrange("(t p) n -> p t n", p=P))\
                      .then_inc(xin_in[h].sem, 16)
                load_gain(g_mem[:], "mem_norm_g")
                load_w(l, 0, kpn(lay(w["w_mem_kv"], l)[:, :, 0:CW]), CW)
                load_gain(g_n1[:], "norm1_g")
                for t, name in ((g_head[:, 0, :], "a_q_norm"),
                                (g_head[:, 1, :], "a_k_norm"), (g_head[:, 2, :], "c_q_norm"),
                                (g_head[:, 3, :], "c_k_norm"), (g_head[:, 4, :], "x_q_norm"),
                                (g_head[:, 5, :], "x_k_norm"), (g_b[:, 0, :], "b_q_norm"),
                                (g_b[:, 1, :], "b_k_norm"), (g_bc[:, 0:QR], "b_q_a_norm"),
                                (g_bc[:, QR:QR + KVR], "b_kv_a_norm")):
                    load_gain(t, name)
                load_w(l, 1, kpn(lay(w["w_mem_kv"], l)[:, :, CW:2 * CW]), CW)
                sp.wait_ge(s_x0, 16)
                sp.dma_start(xin[:, MT:, :], x_acc[:, :].rearrange("(t p) n -> p t n", p=P)).then_inc(xin_in[2].sem, 16)
                sp.dma_start(sinks[:], gains["c_sink"][bass.ds(l, 1), :].to_broadcast([P, 8])).then_inc(g2_in.sem, 16)
                sp.dma_start(wr[:], kpn(lay(w["w_router"], l))).then_inc(g2_in.sem, 16)
                for t, src in ((cosA, "cosA"), (sinA, "sinA")):
                    sp.dma_start(t[:], tables[src]).then_inc(tabA_in.sem, 16)
                load_z(l, "A", 0)
                load_z(l, "A", 1)
                load_z(l, "A", 2)

                def load_cx(i):
                    c = IN_C + i * CW
                    load_w(l, CX0 + i, kpn(lay(w["w_in"], l)[:, :, c:c + CW]), CW)

                def load_pair(i):
                    sp.wait_ge(bp_mm.sem, bp_mm.at(l, i * NT - 1))
                    sp.dma_start(wqp[:], kpn(lay(w["b_w_q_b"], l)[:, :, i * 2 * BQK:(i + 1) * 2 * BQK]))\
                      .then_inc(bw_in[0].sem, 16)
                    sp.dma_start(wkvp[:], kpn(lay(w["b_w_kv_b"], l)[:, :, i * 4 * HD:(i + 1) * 4 * HD]))\
                      .then_inc(bw_in[1].sem, 16)

                for n in range(3):
                    load_z(l, "B", n)
                load_cx(0)
                load_cx(1)
                load_pair(0)
                with sp.Fori(0, BR["A"].its) as it:
                    store_pairs(l, BR["A"], it)

                def load_gate(n, b):
                    j = GATE0 + 4 * n + b
                    slot = b % 2
                    c = sp.snap(n * CW + IN_G + b * D)
                    sp.wait_ge(lo_made.sem, lo_made.at(l, j - 2))
                    sp.dma_start(wraw[:, slot, :].rearrange("p (k n) -> p k n", n=CW),
                                 kpn(lay(w["w_in"], l)[:, :, bass.ds(c, CW)])).then_inc(w_in_slot[slot].sem, 16)

                for i in range(BR["B"].its):
                    if i < 2:
                        load_cx(i + 2)
                    else:
                        load_gate(0, i - 2)
                    if i < 3:
                        load_pair(i + 1)
                    store_pairs(l, BR["B"], i)
                with sp.Fori(0, BR["C"].its) as it:
                    store_pairs(l, BR["C"], it)
                sp.wait_ge(o_out.sem, o_out.at(l, 11))
                sp.sem_inc(passed["sp"], 1)
                sp.wait_ge(prep_t.sem, prep_t.at(l, BR["X"].last_prep(0)))
                sp.dma_start(oT[:, 0:12, :], o_rows[:, :].rearrange("(k p) n -> p k n", p=P)).then_inc(o_in.sem, 16)

                def load_direct(before, k0, slot, rows, k):
                    sp.wait_ge(before.sem, before.at(l, k0))
                    sp.dma_start(wdir[:, slot, 0:k * CW].rearrange("p (k n) -> p k n", n=CW), rows)\
                      .then_inc(d_in[slot].sem, 16)

                def gate_loads(n, last):
                    c = sp.snap(n * CW)
                    load_direct(gate_mm, n * 24 - 13, 0, kpn(lay(w["w_branch"], l)[:, 0:1024, bass.ds(c, CW)]), 8)
                    for b in range(2):
                        load_gate(n, b + 2)
                    c = sp.snap(n * CW)
                    sp.wait_ge(o_ev.sem, o_ev.at(l, 27))
                    sp.sem_inc(passed["sp"], 1)
                    load_direct(gate_mm, n * 24 - 1, 1, kpn(lay(w["w_branch"], l)[:, 1024:1792, bass.ds(c, CW)]), 6)
                    if not last:
                        for b in range(2):
                            load_gate(n + 1, b)

                with sp.Fori(0, 3) as n:
                    gate_loads(n, False)
                gate_loads(3, True)
                for c in range(2):
                    load_direct(gate_mm, 83 + 12 * c, c, kpn(lay(w["w_out"], l)[:, :, c * CW:(c + 1) * CW]), 8)
                sp.wait_ge(gate_mm.sem, gate_mm.at(l, 95))
                sp.dma_start(X2[:], x_acc[:, :].rearrange("(t p) n -> p t n", p=P)).then_inc(x_in2.sem, 16)
                sp.dma_start(g_n2[:], gains["norm2_g"][bass.ds(l, 1), :].to_broadcast([P, D])).then_inc(gn2_in.sem, 16)

                def m_src(e, pos):
                    if pos < 8:
                        col = [0, DE, 512, DE + 512][pos // 2]
                        t = w["w_gate_up"][bass.ds(e, 1), (pos % 2) * 512:(pos % 2 + 1) * 512, col:col + 512]
                    else:
                        r, c = (pos - 8) // 2 * 512, (pos - 8) % 2 * 512
                        t = w["w_down"][bass.ds(e, 1), r:r + 512, c:c + 512]
                    return kpn(t)

                def load_m(e, pos):
                    ex = sp.snap(l * NE + e)
                    sp.dma_start(mraw[:, pos % MSLOTS, :].rearrange("p (k n) -> p k n", n=512), m_src(ex, pos))\
                      .then_inc(m_in_slot[pos % MSLOTS].sem, 16)

                sp.wait_ge(mg_t.sem, mg_t.at(l, 15))
                for pos in range(MSLOTS):
                    load_m(0, pos)
                for c in range(2, 4):
                    load_direct(out_mm, 6 * c - 7, c % 2, kpn(lay(w["w_out"], l)[:, :, c * CW:(c + 1) * CW]), 8)

                def m_loads(e, last):
                    for pos in range(MPOS):
                        if pos < MPOS - MSLOTS:
                            ex = sp.snap(l * NE + e)
                            if pos % POOL_EVERY == 0:
                                sp.wait_ge(lo_pool.sem, lo_pool.at(l, e * (MPOS // POOL_EVERY) + pos // POOL_EVERY))
                            else:
                                sp.wait_ge(lo_made.sem, lo_made.at(l, m_lo_index(e, pos)))
                            sp.dma_start(mraw[:, pos % MSLOTS, :].rearrange("p (k n) -> p k n", n=512),
                                         m_src(ex, pos + MSLOTS)).then_inc(m_in_slot[pos % MSLOTS].sem, 16)
                        elif not last:
                            ex = sp.snap(l * NE + e + 1)
                            if pos % POOL_EVERY == 0:
                                sp.wait_ge(lo_pool.sem, lo_pool.at(l, e * (MPOS // POOL_EVERY) + pos // POOL_EVERY))
                            else:
                                sp.wait_ge(lo_made.sem, lo_made.at(l, m_lo_index(e, pos)))
                            sp.dma_start(mraw[:, pos % MSLOTS, :].rearrange("p (k n) -> p k n", n=512),
                                         m_src(ex, pos + MSLOTS - MPOS)).then_inc(m_in_slot[pos % MSLOTS].sem, 16)

                for t in range(NT):
                    sp.wait_ge(r2_normed.sem, r2_normed.at(l, t))
                    sp.dma_start(x_acc[t * P:(t + 1) * P, :], X2[:, t, :]).then_inc(x_out.sem, 16)
                    sp.dma_start(h_rows[t * P:(t + 1) * P, :], H2[:, t % 2, :]).then_inc(h_out[t % 2].sem, 16)
                with sp.Fori(0, NE - 1) as e:
                    m_loads(e, False)
                m_loads(NE - 1, True)

            sp.wait_ge(y_done.sem, y_done.at(DEPTH - 1, NE - 1))
            sp.dma_start(y_prompt, x_acc[0:2 * P, :]).then_inc(s_out, 16)
            sp.dma_start(y_sample, x_acc[2 * P:NTOK, :]).then_inc(s_out, 16)
            sp.wait_ge(s_out, 32)

        @block.gpsimd
        def _(pool):
            for s in signals:
                s.start(pool)
            pool.memset(ones[:], 1.0)
            pool.memset(eps_t[:], EPS)
            pool.drain()
            pool.affine_select(out=ident[:], in_=ones[:], compare_op=ALU.is_equal, fill=0.0, base=0,
                               pattern=[[-1, P]], channel_multiplier=1).then_inc(s_cst, 1)
            pool.wait_ge(xin_in[1].sem, (LEAD + 1) * 16)
            pool.dma_start(x_acc[:, :], x_in).then_inc(s_x0, 16)
            for t, src in ((cosB, "cosB"), (sinB, "sinB"), (ndist, "ndist"), (slopes, "slopes")):
                pool.dma_start(t[:], tables[src]).then_inc(s_tab, 16)
            def norm_p(l, br, it):
                nu = len(br.units)
                for u, (h, s, t, last) in enumerate(br.units):
                    pool.wait_ge(p_rec.sem, p_rec.at(l, br.unit0 + it * nu + u))
                    pool.sem_inc(passed["pool"], 1)
                    n = br.window(u)[1] * P
                    pool.tensor_scalar(PR[:, u % 3, 0:n], PR[:, u % 3, 0:n], prec[:, u % 4:u % 4 + 1], 1.0,
                                       ALU.mult, ALU.mult).then_inc(p_norm.sem, 1)

            def lo_by_pool(l, e, pos):
                pool.wait_ge(hi_made.sem, hi_made.at(l, NGEMM + e * MPOS + pos))
                pool.tensor_tensor(m_lo(pos), mraw[:, pos % MSLOTS, :], m_hi(pos), ALU.subtract)\
                    .then_inc(lo_pool.sem, 1)

            with pool.Fori(0, DEPTH) as l:
                for name in "ABC":
                    with pool.Fori(0, BR[name].its) as it:
                        norm_p(l, BR[name], it)
                norm_p(l, BR["X"], 0)

                def gather(e, col):
                    pool.tensor_copy(ig[:], idxT[:, bass.ds(col, 1)]).then_inc(ig_ok.sem, 1)
                    pool.wait_ge(ig_ok.sem, ig_ok.at(l, e))
                    pool.sem_inc(passed["pool"], 1)
                    pool.indirect_dma_start(XS[:], None, h_rows[:, :], bass.IndirectOffsetOnAxis(ap=ig[:], axis=0))\
                        .then_inc(xs_in.sem, 16)

                pool.wait_ge(top_ev.sem, top_ev.at(l, 0))
                pool.sem_inc(passed["pool"], 1)
                for i in range(2):
                    pool.wait_ge(h_out[i].sem, h_out[i].at(l, 2))
                    pool.sem_inc(passed["pool"], 1)
                pool.wait_ge(x_out.sem, x_out.at(l, 5))
                pool.sem_inc(passed["pool"], 1)
                gather(0, 0)
                lo_by_pool(l, 0, 0)

                def expert(e, first, last):
                    lo_by_pool(l, e, 3)
                    if not last:
                        col = 1 if first else pool.snap(e + 1)
                        pool.wait_ge(xs_t.sem, xs_t.at(l, 2 * e + 1))
                        pool.sem_inc(passed["pool"], 1)
                        gather(e + 1, col)
                    if not first:
                        pool.wait_ge(y_out.sem, y_out.at(l, e - 1))
                        pool.sem_inc(y_done.sem, 1)
                    for pos in range(2 * POOL_EVERY, MPOS, POOL_EVERY):
                        lo_by_pool(l, e, pos)
                    if not last:
                        lo_by_pool(l, e + 1, 0)
                    col = e if first or last else pool.snap(e)
                    pool.tensor_copy(isc[:], idxT[:, bass.ds(col, 1)]).then_inc(isc_ok.sem, 1)
                    pool.wait_ge(isc_ok.sem, isc_ok.at(l, e))
                    pool.sem_inc(passed["pool"], 1)
                    pool.wait_ge(y_ev.sem, y_ev.at(l, 2 * e + 1))
                    pool.sem_inc(passed["pool"], 1)
                    pool.indirect_dma_start(x_acc[:, :], bass.IndirectOffsetOnAxis(ap=isc[:], axis=0), YS[:], None,
                                            compute_op=ALU.add).then_inc(y_out.sem, 16)
                    if last:
                        pool.wait_ge(y_out.sem, y_out.at(l, e))
                        pool.sem_inc(y_done.sem, 1)

                expert(0, True, False)
                with pool.Fori(1, NE - 1) as e:
                    expert(e, False, False)
                expert(NE - 1, False, True)

        @block.scalar
        def _(act):
            def hi_gemm(l, slot, k, used, last_use):
                act.wait_ge(w_in_slot[slot].sem, w_in_slot[slot].at(l, k))
                act.wait_ge(used.sem, used.at(l, last_use))
                act.activation(whi[:, slot, :], wraw[:, slot, :], ACT.Copy).then_inc(hi_made.sem, 1)

            def hi_moe(l, e, pos):
                act.wait_ge(m_in_slot[pos % MSLOTS].sem, m_in_slot[pos % MSLOTS].at(l, 2 * e + pos // MSLOTS))
                act.wait_ge(m_used.sem, m_used.at(l, e * MPOS + pos - WSLOTS))
                act.activation(m_hi(pos), mraw[:, pos % MSLOTS, :], ACT.Copy).then_inc(hi_made.sem, 1)

            def row_roots(i0, n):
                for i in range(i0, i0 + n):
                    act.activation(nscr[:], xin[:, i, :], ACT.Square, accum_out=row_ss[:, i:i + 1])
                    act.drain()
                act.activation(row_rt[:, i0:i0 + n], row_ss[:, i0:i0 + n], ACT.Sqrt, bias=eps_t[:, 0:1],
                               scale=1.0 / D).then_inc(row_root.sem, 1)

            def row_high(l, i):
                act.wait_ge(row_turned.sem, row_turned.at(l, i))
                c = (i if i < MT else i - MT) * P
                for h in range(2):
                    ins = act.activation(hT_hi[:, 4 * h:4 * h + 4, c:c + P],
                                         row_bank(i, h)[:].rearrange("p (k n) -> p k n", k=4), ACT.Copy)
                ins.then_inc(row_hi.sem, 1)

            def z_copy(l, j, t):
                g = (j - 2) * NT + t
                act.wait_ge(z_mm.sem, z_mm.at(l, g))
                b = bank[g % 4]
                if j < 5:
                    act.activation(Z[:, j - 2, t, :], b[:, 0:256], ACT.Copy).then_inc(z_ev.sem, 1)
                elif j < 7:
                    act.activation(ZB[:, t, (j - 5) * 256:(j - 4) * 256], b[:, 0:256], ACT.Copy).then_inc(z_ev.sem, 1)
                else:
                    act.activation(ZB[:, t, 512:640], b[:, 0:128], ACT.Copy)
                    act.activation(krope[:, t, :], b[:, 128:160], ACT.Copy).then_inc(z_ev.sem, 1)

            def z_high(l, j):
                hi_gemm(l, j % 2, j // 2, *((mem_mm, 2 * MT - 1) if j == 3 else (z_mm, (j - 4) * NT + NT - 1)))

            def squares(parts):
                for out, in_ in parts:
                    ins = act.activation(out, in_, ACT.Square)
                ins.then_inc(pq_sq.sem, 1)

            def roots(l, parts, k):
                act.wait_ge(pq_sum.sem, pq_sum.at(l, k))
                for out, count in parts:
                    ins = act.activation(out, out, ACT.Sqrt, bias=eps_t[:, 0:1], scale=1.0 / count)
                ins.then_inc(pq_root.sem, 1)

            def prep_copies(l, k0, parts):
                for i, (dst, rows, cols) in enumerate(parts):
                    act.wait_ge(prep_t.sem, prep_t.at(l, k0 + i))
                    act.activation(dst, prep_banks[i % 4][0:rows, 0:cols], ACT.Copy)\
                       .then_inc(prep_ev.sem, 1)

            sq_b = cT[:].rearrange("p k n -> p (k n)")

            def bc_squares(t):
                q, kv = t * (QR + KVR), t * (QR + KVR) + QR
                act.activation(sq_b[:, q:q + QR], ZB[:, t, 0:QR], ACT.Square, accum_out=stat[:, t:t + 1])
                act.activation(sq_b[:, kv:kv + KVR], ZB[:, t, QR:QR + KVR], ACT.Square,
                               accum_out=stat[:, NT + t:NT + t + 1])

            def bc_roots():
                act.drain()
                act.activation(stat[:, 0:NT], stat[:, 0:NT], ACT.Sqrt, bias=eps_t[:, 0:1], scale=1.0 / QR)
                act.activation(stat[:, NT:2 * NT], stat[:, NT:2 * NT], ACT.Sqrt, bias=eps_t[:, 0:1], scale=1.0 / KVR)\
                   .then_inc(bc_root.sem, 1)

            def attend(l, br, it):
                nu = len(br.units)
                u0 = br.unit0 + it * nu

                def exps(u):
                    h, s, t, last = br.units[u]
                    n = br.window(u)[1] * P
                    act.wait_ge(sc_max.sem, sc_max.at(l, u0 + u))
                    if br.name == "C":
                        src = PR[:, u % 3, 0:n]
                        act.activation(esink[:, u % 4:u % 4 + 1], it_sink[:, h:h + 1], ACT.Exp,
                                       bias=nmax[:, u % 4:u % 4 + 1])
                    else:
                        act.wait_ge(p_turn.sem, p_turn.at(l, u0 + u - 3))
                        src = score_banks[u % 4][:, 0:n]
                    act.activation(PR[:, u % 3, 0:n], src, ACT.Exp, bias=nmax[:, u % 4:u % 4 + 1],
                                   accum_out=psums[:, u % 4:u % 4 + 1]).then_inc(p_exp.sem, 1)

                exps(0)
                exps(1)
                for u, (h, s, t, last) in enumerate(br.units):
                    if u + 2 < nu:
                        exps(u + 2)
                    act.wait_ge(p_turn.sem, p_turn.at(l, u0 + u))
                    t0, _ = SEQS[s]
                    if t == t0:
                        act.wait_ge(pv_mm.sem, pv_mm.at(l, br.hs0 + it * (2 * br.heads) + br.hs(u) - 2))
                    k0, n = br.window(u)
                    act.activation(PT[:, br.hs(u) % 2, k0:k0 + n, (t - t0) * P:(t - t0 + 1) * P],
                                   bank[3 + u % 2][:, 0:n * P].rearrange("p (k n) -> p k n", k=n), ACT.Copy)\
                       .then_inc(p_ev.sem, 1)
                    if br.name == "A" and it == 1 and 2 <= u < 2 + NT:
                        bc_squares(u - 2)
                    if br.name == "A" and it == 1 and u == 2 + NT:
                        bc_roots()

            def squares_ac():
                act.activation(sq_q, zq, ACT.Square)
                act.activation(sq_k, zk, ACT.Square).then_inc(pq_sq.sem, 1)

            def turned_ac(l, br, it):
                prep_copies(l, it * br.nprep + br.prep0,
                            [(QT[:, j, c:c + n], P, n) for j in range(2) for c, n in ((0, 512), (512, 256))]
                            + [(KT[:, 0, c:c + n], P, n) for c, n in ((0, 512), (512, 256))])

            act.wait_ge(s_cst, 1)
            with act.Fori(0, DEPTH) as l:
                for h in range(2):
                    act.wait_ge(xin_in[h].sem, xin_in[h].at(l, 0))
                    act.sem_inc(passed["act"], 1)
                row_roots(0, MT)
                hi_gemm(l, 0, 0, m_used, -WSLOTS)
                for i in range(MT):
                    row_high(l, i)
                hi_gemm(l, 1, 0, m_used, 1 - WSLOTS)
                act.wait_ge(xin_in[2].sem, xin_in[2].at(l, 0))
                act.sem_inc(passed["act"], 1)
                row_roots(MT, NT)
                for c in range(2):
                    if c == 1:
                        hi_gemm(l, 0, 1, mem_mm, MT - 1)
                    for m in range(MT):
                        g = c * MT + m
                        act.wait_ge(mem_mm.sem, mem_mm.at(l, g))
                        act.activation(mkv[:, m, c * CW:(c + 1) * CW], bank[4 + g % 4][:, 0:CW], ACT.Copy)\
                           .then_inc(mem_ev.sem, 1)
                z_high(l, 3)
                for i in range(2):
                    row_high(l, MT + i)
                for t in range(NT):
                    z_copy(l, 2, t)
                    if t + 2 < NT:
                        row_high(l, MT + t + 2)
                for j in range(3, 5):
                    z_high(l, j + 1)
                    for t in range(NT):
                        z_copy(l, j, t)
                act.drain()
                squares_ac()
                for j in range(5, 8):
                    z_high(l, j + 1)
                    for t in range(NT):
                        z_copy(l, j, t)
                        if j == 5 and t == 1:
                            roots(l, [(stat[:, 0:60], HD)], PREP_A)
                act.drain()
                for it in range(BR["A"].its):
                    turned_ac(l, BR["A"], it)
                    attend(l, BR["A"], it)
                prep_copies(l, B_CPREP0, [(cT[:, k, c:c + n], P, n) for k in range(5) for c, n in ((0, 512), (512, 256))])
                br = BR["B"]
                with act.Fori(0, br.its // 2) as i2:
                    for sub in range(2):
                        it = i2 * 2 + sub
                        hi_gemm(l, (CX0 + 1 + sub) % 2, i2 + (CX0 + 1 + sub) // 2, z_mm, it * NT + ((CX0 - 3) * NT + NT - 1))
                        for t in range(NT):
                            act.wait_ge(bp_mm.sem, bp_mm.at(l, it * NT + t))
                            b = bank[1 + t % 2]
                            kv = b[:, 256:512].rearrange("p (h c) -> p h c", h=2)
                            act.activation(QS[:, t * 2 * BQK:(t + 1) * 2 * BQK], b[:, 0:2 * BQK], ACT.Copy)
                            act.activation(KS[:, t * 2 * BQK:(t + 1) * 2 * BQK].rearrange("p (h c) -> p h c", h=2)[:, :, 0:HD],
                                           kv[:, :, 0:HD], ACT.Copy)
                            act.activation(VS[:, t, :].rearrange("p (h c) -> p h c", h=2), kv[:, :, HD:2 * HD], ACT.Copy)\
                               .then_inc(bp_ev.sem, 1)
                        n = 2 * NT * BQK
                        act.drain()
                        act.wait_ge(krope_in.sem, krope_in.at(l, it))
                        squares([(SQ[:, 0:n], QS[:, 0:n]), (SQ[:, n:2 * n], KS[:, 0:n])])
                        for t in range(NT):
                            act.wait_ge(z_mm.sem, z_mm.at(l, it * NT + ((CX0 - 2) * NT + t)))
                            act.sem_inc(passed["act"], 1)
                            c = act.snap(it)
                            act.activation(Z[:, bass.ds(c, 1), t, :], bank[3 + t % 4][:, 0:256].unsqueeze(1), ACT.Copy)\
                               .then_inc(z_ev.sem, 1)
                            if t == 1:
                                roots(l, [(stat[:, 0:24], BQK)], it + PREP_BP)
                        prep_copies(l, it * br.nprep + br.prep0,
                                    [(T[0:BQK, h, c:c + n], BQK, n) for T in (QT, KT) for h in range(2)
                                     for c, n in ((0, 512), (512, 256))])
                        attend(l, br, it)
                act.wait_ge(pv_mm.sem, pv_mm.at(l, BR["C"].hs0 - 1))
                squares_ac()
                roots(l, [(stat[:, 0:60], HD)], PREP_C)
                for it in range(BR["C"].its):
                    turned_ac(l, BR["C"], it)
                    attend(l, BR["C"], it)
                act.wait_ge(pv_mm.sem, pv_mm.at(l, BR["X"].hs0 - 1))
                squares([(SQ[:, 0:NT * 256].rearrange("p (t c) -> p t c", t=NT), Z[:, 3, :, :]),
                            (SQ[:, NT * 256:(NT + MT) * 256].rearrange("p (t c) -> p t c", t=MT), mkv[:, :, 0:256])])
                roots(l, [(stat[:, 0:40], HD)], PREP_X)
                br = BR["X"]
                prep_copies(l, br.prep0, [(QT[:, j, c:c + n], P, n) for j in range(2) for c, n in ((0, 512), (512, 256))]
                            + [(KT[:, j, 0:512], P, 512) for j in range(2)])
                attend(l, br, 0)

                def gates(n, last):
                    for b in range(4):
                        if not (last and b == 3):
                            hi_gemm(l, (b + 1) % 2, n * 2 + (GATE0 + b + 1) // 2,
                                    gate_mm, n * 24 + (b * NT - 1))
                        for t in range(NT):
                            g = b * NT + t
                            act.wait_ge(gate_mm.sem, gate_mm.at(l, n * 24 + g))
                            act.wait_ge(gate_mg.sem, gate_mg.at(l, n * 24 + g - 2))
                            act.activation(sgb[:, g % 2, :], bank[g % 2][:, 0:CW], ACT.Sigmoid).then_inc(gate_sg.sem, 1)
                    for h in range(2):
                        for i, (c, w_) in enumerate(((0, 512), (512, 256))):
                            act.wait_ge(mg_t.sem, mg_t.at(l, n * 4 + 2 * h + i))
                            act.sem_inc(passed["act"], 1)
                            k = act.snap(n * 2 + h) if not last else 2 * n + h
                            dst = mT[:, bass.ds(k, 1), c:c + w_] if not last else mT[:, k:k + 1, c:c + w_]
                            act.activation(dst, bank[6 + i][:, 0:w_].unsqueeze(1), ACT.Copy).then_inc(mg_ev.sem, 1)

                with act.Fori(0, 3) as n:
                    gates(n, False)
                gates(3, True)

                def mean_square(t):
                    act.wait_ge(out_ev.sem, out_ev.at(l, 18 + t))
                    act.activation(nscr2[:], X2[:, t, :], ACT.Square, accum_out=row_ss[:, t % 2:t % 2 + 1])
                    act.drain()
                    act.activation(row_rt[:, t % 2:t % 2 + 1], row_ss[:, t % 2:t % 2 + 1], ACT.Sqrt, bias=eps_t[:, 0:1],
                                   scale=1.0 / D).then_inc(r2_root.sem, 1)

                mean_square(0)
                mean_square(1)
                for t in range(NT):
                    act.wait_ge(rl_mm.sem, rl_mm.at(l, t - 1))
                    for h in range(2):
                        act.wait_ge(r2_turn.sem, r2_turn.at(l, 2 * t + h))
                        act.activation(H2T[:, 4 * h:4 * h + 4, :], bank[4 + h][:].rearrange("p (k n) -> p k n", k=4),
                                       ACT.Copy).then_inc(r2_ev.sem, 1)
                    if t + 2 < NT:
                        mean_square(t + 2)
                    act.wait_ge(rl_max.sem, rl_max.at(l, t))
                    act.activation(lg[:, t, :], bank[6][:, 0:NE], ACT.Exp, bias=rst[:, t, 0:1],
                                   accum_out=rst[:, t, 1:2]).then_inc(rl_exp.sem, 1)
                for pos in range(AHEAD):
                    hi_moe(l, 0, pos)

                def part_copies(l, turned, k, b, dst, done):
                    act.wait_ge(turned.sem, turned.at(l, k))
                    act.activation(dst, bank[b][:, 0:4 * CAP].rearrange("p (k n) -> p k n", k=4), ACT.Copy)\
                       .then_inc(done.sem, 1)

                for h in range(2):
                    part_copies(l, xs_t, h, 7, xsT_hi[:, 4 * h:4 * h + 4, :], xs_hi)

                def expert(e, last):
                    for pos in range(MPOS):
                        if pos + AHEAD < MPOS:
                            hi_moe(l, e, pos + AHEAD)
                        elif not last:
                            hi_moe(l, e + 1, pos + AHEAD - MPOS)
                        if pos in (1, 5):
                            i = pos // 4
                            act.wait_ge(m_used.sem, m_used.at(l, MPOS * e + 4 * i + 1))
                            act.wait_ge(act_ok.sem, act_ok.at(l, 2 * e + i - 2))
                            act.activation(sg[:, i, :], bank[2 * i][0:CAP, :], ACT.Silu).then_inc(silu_ok.sem, 1)
                        if pos in (5, 8):
                            i = pos // 8
                            part_copies(l, a_t, 2 * e + i, 6, aT_hi[:, 4 * i:4 * i + 4, :], a_hi)
                        if pos in (7, 9) and not last:
                            i = pos // 9
                            part_copies(l, xs_t, 2 * e + 2 + i, 7, xsT_hi[:, 4 * i:4 * i + 4, :], xs_hi)

                with act.Fori(0, NE - 1) as e:
                    expert(e, False)
                expert(NE - 1, True)

        @block.vector
        def _(dve):
            def lo_gemm(l, j, slot):
                dve.wait_ge(hi_made.sem, hi_made.at(l, j))
                dve.tensor_tensor(wlo[:, slot, :], wraw[:, slot, :], whi[:, slot, :], ALU.subtract)\
                   .then_inc(lo_made.sem, 1)

            def lo_moe(l, e, pos):
                dve.wait_ge(hi_made.sem, hi_made.at(l, NGEMM + e * MPOS + pos))
                dve.tensor_tensor(m_lo(pos), mraw[:, pos % MSLOTS, :], m_hi(pos), ALU.subtract)\
                   .then_inc(lo_made.sem, 1)

            def row_norm(l, i):
                dve.scalar_tensor_tensor(out=xin[:, i, :], in0=xin[:, i, :], scalar=row_rt[:, i:i + 1],
                                         in1=(g_mem if i < MT else g_n1)[:], op0=ALU.mult, op1=ALU.mult)\
                   .then_inc(row_normed.sem, 1)

            def row_low(l, i):
                dve.wait_ge(row_hi.sem, row_hi.at(l, i))
                c = (i if i < MT else i - MT) * P
                for h in range(2):
                    ins = dve.tensor_tensor(hT_lo[:, 4 * h:4 * h + 4, c:c + P],
                                            row_bank(i, h)[:].rearrange("p (k n) -> p k n", k=4),
                                            hT_hi[:, 4 * h:4 * h + 4, c:c + P], ALU.subtract)
                ins.then_inc(row_lo.sem, 1)

            def inv_row_roots(l, i0, n, k):
                dve.wait_ge(row_root.sem, row_root.at(l, k))
                dve.reciprocal(row_rt[:, i0:i0 + n], row_rt[:, i0:i0 + n])
                dve.drain()

            def inv_roots(l, k, parts):
                dve.wait_ge(pq_sq.sem, pq_sq.at(l, k))
                for c, n, size, src in parts:
                    ins = dve.tensor_reduce(stat[:, c:c + n], src, AX.X, ALU.add)
                ins.then_inc(pq_sum.sem, 1)
                dve.wait_ge(pq_root.sem, pq_root.at(l, k))
                n = parts[-1][0] + parts[-1][1]
                dve.reciprocal(stat[:, 0:n], stat[:, 0:n])
                dve.drain()

            def by_stat(t, c, tiles, groups, size):
                v = t.rearrange("p t (g d) -> p t g d", g=groups)
                r = stat[:, c:c + tiles * groups].rearrange("p (t g) -> p t g", t=tiles)
                dve.tensor_tensor(v, v, r.unsqueeze(3).to_broadcast([P, tiles, groups, size]), ALU.mult)

            def by_gain(t, gain, tiles, groups, size):
                v = t.rearrange("p t (g d) -> p t g d", g=groups)
                g = gain.unsqueeze(1).unsqueeze(1).to_broadcast([P, tiles, groups, size])
                dve.tensor_tensor(v, v, g, ALU.mult)

            def rope_a(z, tiles, groups):
                n = tiles * groups * HD
                v = z.rearrange("p t (g d) -> p t g d", g=groups)
                own = SQ[:, 0:n].rearrange("p (t g d) -> p t g d", t=tiles, g=groups)
                other = SQ[:, n:2 * n].rearrange("p (t g d) -> p t g d", t=tiles, g=groups)
                dve.tensor_tensor(own, v, cosA[:].unsqueeze(2).to_broadcast([P, tiles, groups, HD]), ALU.mult)
                for a in range(4):
                    to, of = slice(16 * a, 16 * a + 16), slice(16 * (a ^ 1), 16 * (a ^ 1) + 16)
                    dve.tensor_tensor(other[:, :, :, to], v[:, :, :, of],
                                      sinA[:, :, to].unsqueeze(2).to_broadcast([P, tiles, groups, 16]), ALU.mult)
                dve.drain()
                dve.tensor_tensor(v, own, other, ALU.add)
                dve.drain()

            def rope_b(T, o):
                v = T[:, 0:2 * NT * BQK].rearrange("p (g d) -> p g d", g=2 * NT)[:, :, HD:BQK]
                own = SQ[:, o:o + 2 * NT * ROPE].rearrange("p (g d) -> p g d", g=2 * NT)
                other = SQ[:, o + 384:o + 384 + 2 * NT * ROPE].rearrange("p (g d) -> p g d", g=2 * NT)
                dve.tensor_tensor(own, v, cosB[:], ALU.mult)
                for x in range(2):
                    a, b = slice(x * 16, x * 16 + 16), slice((1 - x) * 16, (1 - x) * 16 + 16)
                    dve.tensor_tensor(other[:, :, a], v[:, :, b], sinB[:, :, a], ALU.mult)
                dve.drain()
                dve.tensor_tensor(v, own, other, ALU.add)

            def norms_ac(l, prep, gq, gk, between):
                dve.wait_ge(pq_sq.sem, pq_sq.at(l, prep))
                dve.tensor_reduce(stat[:, 0:48], sq_q.rearrange("p r (g d) -> p (r g) d", d=HD), AX.X, ALU.add)
                dve.tensor_reduce(stat[:, 48:60], sq_k.rearrange("p t (g d) -> p (t g) d", d=HD), AX.X, ALU.add)\
                   .then_inc(pq_sum.sem, 1)
                if between:
                    lo_gemm(l, between, between % 2)
                dve.wait_ge(pq_root.sem, pq_root.at(l, prep))
                dve.reciprocal(stat[:, 0:60], stat[:, 0:60])
                dve.drain()
                by_stat(zq, 0, 12, 4, HD)
                by_stat(zk, 48, NT, 2, HD)
                dve.drain()
                if between:
                    lo_gemm(l, between + 1, (between + 1) % 2)
                by_gain(zq, g_head[:, gq, :], 12, 4, HD)
                by_gain(zk, g_head[:, gk, :], NT, 2, HD)
                dve.drain()

            def double_keys(name):
                twice = k_twice[name].rearrange("p (t h) (c d) -> p t h c d", h=2, c=2)
                for h in range(2):
                    dve.tensor_copy(twice[:, :, h], Z[:, 2, :, h * HD:(h + 1) * HD].unsqueeze(2).to_broadcast([P, NT, 2, HD]))

            def bc_norm(l, t):
                if t == 0:
                    dve.wait_ge(bc_root.sem, bc_root.at(l, 0))
                    dve.reciprocal(stat[:, 0:2 * NT], stat[:, 0:2 * NT])
                    dve.drain()
                dve.scalar_tensor_tensor(out=ZB[:, t, 0:QR], in0=ZB[:, t, 0:QR], scalar=stat[:, t:t + 1],
                                         in1=g_bc[:, 0:QR], op0=ALU.mult, op1=ALU.mult)
                dve.scalar_tensor_tensor(out=ZB[:, t, QR:QR + KVR], in0=ZB[:, t, QR:QR + KVR],
                                         scalar=stat[:, NT + t:NT + t + 1], in1=g_bc[:, QR:QR + KVR],
                                         op0=ALU.mult, op1=ALU.mult)
                if t == NT - 1:
                    dve.drain().then_inc(bc_done.sem, 1)

            def attend(l, br, it):
                nu = len(br.units)
                u0 = br.unit0 + it * nu
                if br.name == "C":
                    c = it * 4
                    dve.tensor_copy(it_slope[:], slopes[:, bass.ds(c, 4)])
                    dve.tensor_copy(it_sink[:], sinks[:, bass.ds(c, 4)])
                    dve.drain()
                    dve.tensor_scalar(it_nsink[:], it_sink[:], -1.0, None, ALU.mult)
                    dve.drain()

                def maxima(u):
                    h, s, t, last = br.units[u]
                    k0, n = br.window(u)
                    n *= P
                    m = slice(u % 4, u % 4 + 1)
                    dve.wait_ge(sc_mm.sem, sc_mm.at(l, u0 + u))
                    if br.name == "C":
                        dve.wait_ge(p_turn.sem, p_turn.at(l, u0 + u - 3))
                        o = (3 - (t - SEQS[s][0]) + k0) * P
                        dve.scalar_tensor_tensor(out=PR[:, u % 3, 0:n], in0=ndist[:, o:o + n], scalar=it_slope[:, h:h + 1],
                                                 in1=score_banks[u % 4][:, 0:n], op0=ALU.mult, op1=ALU.add)
                        dve.drain()
                        dve.tensor_reduce(nraw[:, m], PR[:, u % 3, 0:n], AX.X, ALU.max, negate=True)
                        dve.drain()
                        dve.tensor_tensor(nmax[:, m], nraw[:, m], it_nsink[:, h:h + 1], ALU.min).then_inc(sc_max.sem, 1)
                    else:
                        dve.tensor_reduce(nmax[:, m], score_banks[u % 4][:, 0:n], AX.X, ALU.max, negate=True)\
                           .then_inc(sc_max.sem, 1)

                def outputs(u):
                    h, s, t, last = br.units[u]
                    n = it * (br.heads // 2) + (br.pair0 + h // 2)
                    if br.name == "X":
                        dve.wait_ge(pv_mm.sem, pv_mm.at(l, br.hs0 + br.hs(u)))
                        t0, nt = SEQS[s]
                        dve.tensor_copy(oT[:, 12 + h // 2, t0 * P:(t0 + nt) * P], bank[5 + s][:, 0:nt * P])\
                           .then_inc(o_ev.sem, 1)
                        return
                    dve.wait_ge(pv_mm.sem, pv_mm.at(l, br.hs0 + it * (2 * br.heads) + br.hs(u)))
                    dve.wait_ge(o_out.sem, o_out.at(l, n - 1))
                    t0, nt = SEQS[s]
                    dve.tensor_copy(OS[:, t0 * P:(t0 + nt) * P], bank[5 + s][:, 0:nt * P]).then_inc(o_ev.sem, 1)

                ahead = 2 if br.name == "C" else 3
                for u in range(ahead):
                    maxima(u)
                due = []
                for u, (h, s, t, last) in enumerate(br.units):
                    dve.wait_ge(p_exp.sem, p_exp.at(l, u0 + u))
                    m = slice(u % 4, u % 4 + 1)
                    if br.name == "C":
                        dve.tensor_tensor(psums[:, m], psums[:, m], esink[:, m], ALU.add)
                        dve.drain()
                    dve.reciprocal(prec[:, m], psums[:, m]).then_inc(p_rec.sem, 1)
                    if u + ahead < nu:
                        maxima(u + ahead)
                    if br.name == "A" and it == 1 and 12 <= u < 12 + NT:
                        bc_norm(l, u - 12)
                    if last and h % 2:
                        due.append(u)
                    if due and u >= due[0] + 3:
                        outputs(due.pop(0))
                for u in due:
                    outputs(u)

            dve.wait_ge(s_cst, 1)
            with dve.Fori(0, DEPTH) as l:
                dve.wait_ge(gains_in.sem, gains_in.at(l, 11))
                for i in (0, 2, 4):
                    dve.tensor_scalar(g_head[:, i, :], g_head[:, i, :], HD ** -0.5, None, ALU.mult)
                dve.tensor_scalar(g_b[:, 0, :], g_b[:, 0, :], BQK ** -0.5, None, ALU.mult)
                inv_row_roots(l, 0, MT, 0)
                for i in range(MT):
                    row_norm(l, i)
                lo_gemm(l, 0, 0)
                for i in range(MT):
                    row_low(l, i)
                lo_gemm(l, 1, 1)
                inv_row_roots(l, MT, NT, 1)
                for i in range(MT, MT + NT):
                    row_norm(l, i)
                lo_gemm(l, 2, 0)
                lo_gemm(l, 3, 1)
                for i in range(MT, MT + NT):
                    row_low(l, i)
                for j in range(4, 6):
                    lo_gemm(l, j, j % 2)
                norms_ac(l, PREP_A, 0, 1, 6)
                dve.wait_ge(tabA_in.sem, tabA_in.at(l, 1))
                for c in range(2):
                    rope_a(Z[:, c, :, :], NT, 4)
                rope_a(zk, NT, 2)
                double_keys("A")
                dve.drain().then_inc(pq_done.sem, 1)
                lo_gemm(l, 8, 0)
                for it in range(BR["A"].its):
                    attend(l, BR["A"], it)
                dve.wait_ge(s_tab, 4 * 16)
                br = BR["B"]
                with dve.Fori(0, br.its // 2) as i2:
                    for sub in range(2):
                        it = i2 * 2 + sub
                        lo_gemm(l, it + (CX0 + 1), (CX0 + 1 + sub) % 2)
                        dve.wait_ge(bp_mm.sem, bp_mm.at(l, it * NT))
                        KSv = KS[:].rearrange("p (t h c) -> p t h c", t=NT, h=2)
                        for h in range(2):
                            dve.tensor_copy(KSv[:, :, h, HD:BQK], krope[:])
                        dve.drain().then_inc(krope_in.sem, 1)
                        n = 2 * NT * BQK
                        inv_roots(l, it + PREP_BP,
                                  [(0, 24, BQK, SQ[:, 0:2 * n].rearrange("p (g d) -> p g d", d=BQK))])
                        for i, T in enumerate((QS, KS)):
                            by_stat(T[:, 0:n].unsqueeze(1), 12 * i, 1, 12, BQK)
                        dve.drain()
                        for i, T in enumerate((QS, KS)):
                            by_gain(T[:, 0:n].unsqueeze(1), g_b[:, i, :], 1, 12, BQK)
                        dve.drain()
                        rope_b(QS, 0)
                        rope_b(KS, 768)
                        dve.drain().then_inc(pq_done.sem, 1)
                        attend(l, br, it)
                norms_ac(l, PREP_C, 2, 3, None)
                double_keys("C")
                dve.drain().then_inc(pq_done.sem, 1)
                for it in range(BR["C"].its):
                    attend(l, BR["C"], it)
                inv_roots(l, PREP_X, [(0, 40, HD, SQ[:, 0:40 * HD].rearrange("p (g d) -> p g d", d=HD))])
                by_stat(Z[:, 3, :, :], 0, NT, 4, HD)
                by_stat(mkv[:, :, 0:256], 24, MT, 4, HD)
                dve.drain()
                by_gain(Z[:, 3, :, :], g_head[:, 4, :], NT, 4, HD)
                by_gain(mkv[:, :, 0:256], g_head[:, 5, :], MT, 4, HD)
                dve.drain().then_inc(pq_done.sem, 1)
                attend(l, BR["X"], 0)

                def gates(n, last):
                    for b in range(4):
                        if not (last and b == 3):
                            lo_gemm(l, n * 4 + (GATE0 + b + 1), (b + 1) % 2)
                        for t in range(NT):
                            g = b * NT + t
                            if b == 0 and t == 0:
                                dve.wait_ge(mg_t.sem, mg_t.at(l, n * 4 - 1))
                            dve.wait_ge(gate_sg.sem, gate_sg.at(l, n * 24 + g))
                            prod = bank[2 + g % 2][:, 0:CW]
                            if b == 0:
                                dve.tensor_tensor(mg[:, t, :], sgb[:, g % 2, :], prod, ALU.mult).then_inc(gate_mg.sem, 1)
                            else:
                                dve.tensor_tensor(gpb[:, g % 2, :], sgb[:, g % 2, :], prod, ALU.mult)
                                dve.drain()
                                dve.tensor_tensor(mg[:, t, :], mg[:, t, :], gpb[:, g % 2, :], ALU.add)\
                                   .then_inc(gate_mg.sem, 1)

                with dve.Fori(0, 3) as n:
                    gates(n, False)
                gates(3, True)

                def residual(g):
                    c, t = g // NT, g % NT
                    dve.wait_ge(out_mm.sem, out_mm.at(l, g))
                    x = X2[:, t, c * CW:(c + 1) * CW]
                    dve.tensor_tensor(x, x, bank[g % 4][:, 0:CW], ALU.add).then_inc(out_ev.sem, 1)

                def norm2(t):
                    dve.wait_ge(r2_root.sem, r2_root.at(l, t))
                    dve.reciprocal(row_rt[:, t % 2:t % 2 + 1], row_rt[:, t % 2:t % 2 + 1])
                    dve.drain()
                    dve.wait_ge(r2_turn.sem, r2_turn.at(l, 2 * (t - 2) + 1))
                    if t >= 2:
                        dve.wait_ge(h_out[t % 2].sem, h_out[t % 2].at(l, t // 2 - 1))
                    dve.scalar_tensor_tensor(out=H2[:, t % 2, :], in0=X2[:, t, :], scalar=row_rt[:, t % 2:t % 2 + 1],
                                             in1=g_n2[:], op0=ALU.mult, op1=ALU.mult).then_inc(r2_normed.sem, 1)

                def affinity(t):
                    dve.wait_ge(rl_mm.sem, rl_mm.at(l, t))
                    dve.tensor_reduce(rst[:, t, 0:1], bank[6][:, 0:NE], AX.X, ALU.max, negate=True).then_inc(rl_max.sem, 1)
                    dve.wait_ge(rl_exp.sem, rl_exp.at(l, t))
                    dve.reciprocal(rst[:, t, 2:3], rst[:, t, 1:2])
                    dve.drain()
                    dve.tensor_scalar(lg[:, t, :], lg[:, t, :], rst[:, t, 2:3], None, ALU.mult).then_inc(rl_aff.sem, 1)

                dve.wait_ge(x_in2.sem, x_in2.at(l, 0))
                dve.wait_ge(gn2_in.sem, gn2_in.at(l, 0))
                for g in range(18):
                    residual(g)
                for i in range(NT + 3):
                    if i < NT:
                        residual(18 + i)
                    if 1 <= i <= NT:
                        norm2(i - 1)
                    if i >= 3:
                        affinity(i - 3)
                dve.wait_ge(aff_t.sem, aff_t.at(l, 0))
                dve.tensor_copy(affT[:, 0:256], bank[6][0:NE, 0:256])
                dve.tensor_copy(affT[:, 256:768], bank[7][0:NE, :])
                dve.drain()
                c = 0
                for (t0, nt), cap in zip(SEQS, CAPS):
                    a = affT[:, t0 * P:(t0 + nt) * P]
                    for r in range(cap // 8):
                        v = val[:, c:c + 8]
                        dve.max(v, a)
                        dve.drain()
                        dve.max_index(idu[:, c:c + 8], v, a)
                        if r + 1 < cap // 8:
                            dve.match_replace(a, v, a, -1.0)
                        dve.drain()
                        c += 8
                dve.tensor_copy(idf[:, 0:CAPS[0]], idu[:, 0:CAPS[0]])
                dve.tensor_scalar(idf[:, CAPS[0]:CAP], idu[:, CAPS[0]:CAP], float(SEQS[1][0] * P), None, ALU.add)
                dve.drain().then_inc(top_done.sem, 1)
                dve.wait_ge(top_t.sem, top_t.at(l, 0))
                dve.tensor_copy(valT[:], bank[4][0:CAP, 0:NE])
                dve.tensor_copy(idxT[:], bank[5][0:CAP, 0:NE])
                dve.drain().then_inc(top_ev.sem, 1)

                def low_parts(hi_done, k, b, dst, hi, done):
                    dve.wait_ge(hi_done.sem, hi_done.at(l, k))
                    dve.tensor_tensor(dst, bank[b][:, 0:4 * CAP].rearrange("p (k n) -> p k n", k=4), hi, ALU.subtract)\
                       .then_inc(done.sem, 1)

                for h in range(2):
                    k = slice(4 * h, 4 * h + 4)
                    low_parts(xs_hi, h, 7, xsT_lo[:, k, :], xsT_hi[:, k, :], xs_lo)

                for pos in range(1, AHEAD):
                    lo_moe(l, 0, pos)

                def expert(e, last):
                    for pos in range(MPOS):
                        nxt = pos + AHEAD
                        if nxt % POOL_EVERY:
                            if nxt < MPOS:
                                lo_moe(l, e, nxt)
                            elif not last:
                                lo_moe(l, e + 1, nxt - MPOS)
                        if pos in (3, 7):
                            i = pos // 4
                            dve.wait_ge(m_used.sem, m_used.at(l, MPOS * e + 4 * i + 3))
                            dve.wait_ge(silu_ok.sem, silu_ok.at(l, 2 * e + i))
                            dve.tensor_tensor(act_s[:, i * 512:(i + 1) * 512], sg[:, i, :], bank[2 * i + 1][0:CAP, :],
                                              ALU.mult).then_inc(act_ok.sem, 1)
                        if pos in (5, 8):
                            k = slice(pos // 8 * 4, pos // 8 * 4 + 4)
                            low_parts(a_hi, 2 * e + pos // 8, 6, aT_lo[:, k, :], aT_hi[:, k, :], a_lo)
                        if pos in (7, 9) and not last:
                            k = slice(pos // 9 * 4, pos // 9 * 4 + 4)
                            low_parts(xs_hi, 2 * e + 2 + pos // 9, 7, xsT_lo[:, k, :], xsT_hi[:, k, :], xs_lo)
                        if pos in (10, 11):
                            i = pos - 10
                            ex = dve.snap(e) if not last else e
                            dve.wait_ge(y_done.sem, y_done.at(l, e - 1))
                            dve.wait_ge(m_used.sem, m_used.at(l, MPOS * e + pos))
                            gate = valT[:, bass.ds(ex, 1)] if not last else valT[:, ex:ex + 1]
                            dve.tensor_scalar(YS[:, i * 512:(i + 1) * 512], bank[4 + i][0:CAP, :], gate, None, ALU.mult)\
                               .then_inc(y_ev.sem, 1)

                with dve.Fori(0, NE - 1) as e:
                    expert(e, False)
                expert(NE - 1, True)

        @block.tensor
        def _(pe):
            def product3(out, lhs_hi, lhs_lo, rhs_hi, rhs_lo, first, last):
                pe.matmul(out, lhs_hi, rhs_hi, start=first, stop=False)
                pe.matmul(out, lhs_hi, rhs_lo, start=False, stop=False)
                return pe.matmul(out, lhs_lo, rhs_hi, start=False, stop=last)

            def row_turn(l, i):
                pe.wait_ge(row_normed.sem, row_normed.at(l, i))
                pe.wait_ge(row_lo.sem, row_lo.at(l, i - 2))
                for k in range(KD):
                    ins = pe.transpose(row_bank(i, k // 4)[:, k % 4 * P:(k % 4 + 1) * P],
                                       xin[:, i, k * P:(k + 1) * P], ident[:])
                ins.then_inc(row_turned.sem, 1)

            def group3(out, t, slot, width):
                wh = whi[:, slot, 0:KD * width].rearrange("p (k n) -> p k n", k=KD)
                wl = wlo[:, slot, 0:KD * width].rearrange("p (k n) -> p k n", k=KD)
                c = slice(t * P, (t + 1) * P)
                for k in range(KD):
                    ins = product3(out, hT_hi[:, k, c], hT_lo[:, k, c], wh[:, k, :], wl[:, k, :], k == 0, k == KD - 1)
                return ins

            def z_group(l, j, width, t):
                g = (j - 2) * NT + t
                pe.wait_ge(z_ev.sem, z_ev.at(l, g - 4))
                group3(bank[g % 4][:, 0:width], t, j % 2, width).then_inc(z_mm.sem, 1)

            def z_rows(l, chunks):
                for j, c, width in chunks:
                    pe.wait_ge(lo_made.sem, lo_made.at(l, j))
                    for t in range(NT):
                        z_group(l, j, width, t)

            def turns(l, k0, parts):
                for i, (rows_, srcs) in enumerate(parts):
                    pe.wait_ge(prep_ev.sem, prep_ev.at(l, k0 + i - 4))
                    b = prep_banks[i % 4]
                    for n, src in enumerate(srcs):
                        ins = pe.transpose(b[0:rows_, n * P:(n + 1) * P], src, ident[:])
                    ins.then_inc(prep_t.sem, 1)

            def halves(f):
                return [[f(t) for t in range(0, 4)], [f(t) for t in range(4, NT)]]

            def attend(l, br, it):
                nu = len(br.units)
                u0 = br.unit0 + it * nu
                pe.wait_ge(prep_ev.sem, prep_ev.at(l, it * br.nprep + (br.prep0 + br.nprep - 1)))

                def scores(u):
                    h, s, t, last = br.units[u]
                    pe.wait_ge(p_exp.sem, p_exp.at(l, u0 + u - 4))
                    pe.matmul(score_banks[u % 4][:, 0:br.window(u)[1] * P], br.q(QT, h, t), br.k(KT, u), start=True, stop=True)\
                      .then_inc(sc_mm.sem, 1)

                def turn(u):
                    h, s, t, last = br.units[u]
                    pe.wait_ge(p_norm.sem, p_norm.at(l, u0 + u))
                    pe.wait_ge(p_ev.sem, p_ev.at(l, u0 + u - 2))
                    for k in range(br.window(u)[1]):
                        ins = pe.transpose(bank[3 + u % 2][:, k * P:(k + 1) * P], PR[:, u % 3, k * P:(k + 1) * P], ident[:])
                    ins.then_inc(p_turn.sem, 1)

                def output(u):
                    h, s, t, last = br.units[u]
                    pe.wait_ge(p_ev.sem, p_ev.at(l, u0 + u))
                    n = it * (br.heads // 2) + (br.pair0 + h // 2)
                    if h % 2 == 0:
                        pe.wait_ge(o_ev.sem, o_ev.at(l, 2 * n + s - 2))
                    nq = SEQS[s][1] * P
                    r = h % 2 * HD
                    nk = br.nkt(s)
                    if br.name == "C":
                        for i in range(SEQS[s][1]):
                            k0, n = br.window(u - (SEQS[s][1] - 1) + i)
                            c = slice(i * P, (i + 1) * P)
                            for k in range(k0, k0 + n):
                                ins = pe.matmul(bank[5 + s][r:r + HD, c], v_of(br, h, s, k, it),
                                                PT[:, br.hs(u) % 2, k, c], start=k == k0, stop=k == k0 + n - 1)
                        ins.then_inc(pv_mm.sem, 1)
                        return
                    for k in range(nk):
                        ins = pe.matmul(bank[5 + s][r:r + HD, 0:nq], v_of(br, h, s, k, it), PT[:, br.hs(u) % 2, k, 0:nq],
                                        start=k == 0, stop=k == nk - 1)
                    ins.then_inc(pv_mm.sem, 1)

                for u in range(3):
                    scores(u)
                due = []
                for u, (h, s, t, last) in enumerate(br.units):
                    if u + 3 < nu:
                        scores(u + 3)
                    turn(u)
                    for v in due:
                        output(v)
                    due = [u] if last else []
                for v in due:
                    output(v)

            def heads_ac(l, br, prep):
                pe.wait_ge(pq_done.sem, pq_done.at(l, prep))
                for it in range(br.its):
                    turns(l, it * br.nprep + br.prep0,
                          [(P, x) for j in range(2)
                           for x in halves(lambda t: Z[:, it, t, j * P:(j + 1) * P])]
                          + [(P, x) for x in halves(lambda t: k_twice[br.name][:, 2 * t + it, :])])
                    attend(l, br, it)

            pe.wait_ge(s_cst, 1)
            with pe.Fori(0, DEPTH) as l:
                for i in range(MT):
                    row_turn(l, i)
                for c in range(2):
                    pe.wait_ge(lo_made.sem, lo_made.at(l, c))
                    for m in range(MT):
                        g = c * MT + m
                        if c == 0:
                            pe.wait_ge(row_lo.sem, row_lo.at(l, m))
                        pe.wait_ge(mem_ev.sem, mem_ev.at(l, g - 4))
                        group3(bank[4 + g % 4][:, 0:CW], m, c, CW).then_inc(mem_mm.sem, 1)
                pe.wait_ge(mem_ev.sem, mem_ev.at(l, 2 * MT - 1))
                for i in range(2):
                    row_turn(l, MT + i)
                pe.wait_ge(lo_made.sem, lo_made.at(l, 2))
                for t in range(NT):
                    pe.wait_ge(row_lo.sem, row_lo.at(l, MT + t))
                    z_group(l, 2, CW, t)
                    if t + 2 < NT:
                        row_turn(l, MT + t + 2)
                z_rows(l, Z_CHUNKS["A"][1:])
                z_rows(l, Z_CHUNKS["B"])
                pe.wait_ge(z_ev.sem, z_ev.at(l, 6 * NT - 1))
                heads_ac(l, BR["A"], PREP_A)
                pe.wait_ge(bc_done.sem, bc_done.at(l, 0))
                turns(l, B_CPREP0, [(P, x) for k in range(5) for x in halves(lambda t: ZB[:, t, k * P:(k + 1) * P])])
                pe.wait_ge(prep_ev.sem, prep_ev.at(l, B_CPREP0 + 9))
                pe.sem_inc(passed["pe"], 1)
                br = BR["B"]
                with pe.Fori(0, br.its // 2) as i2:
                    for sub in range(2):
                        it = i2 * 2 + sub
                        pe.wait_ge(bw_in[0].sem, bw_in[0].at(l, it))
                        pe.wait_ge(bw_in[1].sem, bw_in[1].at(l, it))
                        for t in range(NT):
                            b = bank[1 + t % 2]
                            pe.wait_ge(bp_ev.sem, bp_ev.at(l, it * NT + (t - 2)))
                            c = slice(t * P, (t + 1) * P)
                            for k in range(3):
                                pe.matmul(b[:, 0:2 * BQK], cT[:, k, c], wqp[:, k, :], start=k == 0, stop=k == 2)
                            for k in range(2):
                                ins = pe.matmul(b[:, 256:512], cT[:, 3 + k, c], wkvp[:, k, :], start=k == 0, stop=k == 1)
                            ins.then_inc(bp_mm.sem, 1)
                        pe.wait_ge(lo_made.sem, lo_made.at(l, it + CX0))
                        pe.wait_ge(o_ev.sem, o_ev.at(l, 2 * it + (2 * br.pair0 - 1)))
                        for t in range(NT):
                            if t >= 4:
                                pe.wait_ge(z_ev.sem, z_ev.at(l, it * NT + ((CX0 - 2) * NT + t - 4)))
                            group3(bank[3 + t % 4][:, 0:CW], t, (CX0 + sub) % 2, CW).then_inc(z_mm.sem, 1)
                        pe.wait_ge(pq_done.sem, pq_done.at(l, it + PREP_BP))

                        def head(T, h):
                            return halves(lambda t: T[:, t * 2 * BQK + h * BQK:t * 2 * BQK + (h + 1) * BQK])

                        turns(l, it * br.nprep + br.prep0, [(BQK, x) for T in (QS, KS) for h in range(2) for x in head(T, h)])
                        attend(l, br, it)
                heads_ac(l, BR["C"], PREP_C)
                pe.wait_ge(pq_done.sem, pq_done.at(l, PREP_X))
                br = BR["X"]
                turns(l, br.prep0,
                      [(P, x) for j in range(2) for x in halves(lambda t: Z[:, 3, t, j * P:(j + 1) * P])]
                      + [(P, [mkv[:, t, j * P:(j + 1) * P] for t in range(MT)]) for j in range(2)])
                attend(l, br, 0)
                pe.wait_ge(o_ev.sem, o_ev.at(l, 27))
                pe.sem_inc(passed["pe"], 1)
                pe.wait_ge(o_in.sem, o_in.at(l, 0))
                pe.sem_inc(passed["pe"], 1)

                def gates(n):
                    for b in range(4):
                        pe.wait_ge(lo_made.sem, lo_made.at(l, n * 4 + (GATE0 + b)))
                        if b % 2 == 0:
                            pe.wait_ge(d_in[b // 2].sem, d_in[b // 2].at(l, n))
                        nk = 2 if b == 3 else 4
                        for t in range(NT):
                            g = b * NT + t
                            pe.wait_ge(gate_mg.sem, gate_mg.at(l, n * 24 + (g - 2)))
                            group3(bank[g % 2][:, 0:CW], t, b % 2, CW)
                            for k in range(nk):
                                kk = b % 2 * 4 + k
                                ins = pe.matmul(bank[2 + g % 2][:, 0:CW], oT[:, 4 * b + k, t * P:(t + 1) * P],
                                                wdir[:, b // 2, kk * CW:(kk + 1) * CW], start=k == 0, stop=k == nk - 1)
                            ins.then_inc(gate_mm.sem, 1)
                    pe.wait_ge(gate_mg.sem, gate_mg.at(l, n * 24 + 23))
                    for h in range(2):
                        for i, ts in enumerate((range(0, 4), range(4, NT))):
                            pe.wait_ge(mg_ev.sem, mg_ev.at(l, n * 4 + (2 * h + i - 2)))
                            for m, t in enumerate(ts):
                                ins = pe.transpose(bank[6 + i][:, m * P:(m + 1) * P], mg[:, t, h * P:(h + 1) * P], ident[:])
                            ins.then_inc(mg_t.sem, 1)

                with pe.Fori(0, 4) as n:
                    gates(n)
                pe.wait_ge(mg_ev.sem, mg_ev.at(l, 15))

                def project(g):
                    c, t = g // NT, g % NT
                    if t == 0:
                        pe.wait_ge(d_in[c % 2].sem, d_in[c % 2].at(l, 4 + c // 2))
                    pe.wait_ge(out_ev.sem, out_ev.at(l, g - 4))
                    for k in range(KD):
                        ins = pe.matmul(bank[g % 4][:, 0:CW], mT[:, k, t * P:(t + 1) * P],
                                        wdir[:, c % 2, k * CW:(k + 1) * CW], start=k == 0, stop=k == KD - 1)
                    ins.then_inc(out_mm.sem, 1)

                def turn_h(t):
                    pe.wait_ge(r2_normed.sem, r2_normed.at(l, t))
                    for h in range(2):
                        pe.wait_ge(r2_ev.sem, r2_ev.at(l, 2 * (t - 1) + h))
                        for k in range(4):
                            kk = 4 * h + k
                            ins = pe.transpose(bank[4 + h][:, k * P:(k + 1) * P], H2[:, t % 2, kk * P:(kk + 1) * P], ident[:])
                        ins.then_inc(r2_turn.sem, 1)

                def route(t):
                    pe.wait_ge(r2_ev.sem, r2_ev.at(l, 2 * t + 1))
                    pe.wait_ge(rl_exp.sem, rl_exp.at(l, t - 1))
                    for k in range(KD):
                        ins = pe.matmul(bank[6][:, 0:NE], H2T[:, k, :], wr[:, k, :], start=k == 0, stop=k == KD - 1)
                    ins.then_inc(rl_mm.sem, 1)

                pe.wait_ge(g2_in.sem, g2_in.at(l, 1))
                for g in range(18):
                    project(g)
                for i in range(NT + 3):
                    if i < NT:
                        project(18 + i)
                    if i >= 3:
                        route(i - 3)
                    if 2 <= i < NT + 2:
                        turn_h(i - 2)
                pe.wait_ge(rl_aff.sem, rl_aff.at(l, NT - 1))
                pe.sem_inc(passed["pe"], 1)
                for t in range(NT):
                    b, c = (bank[6], t) if t < 2 else (bank[7], t - 2)
                    ins = pe.transpose(b[0:NE, c * P:(c + 1) * P], lg[:, t, :], ident[:])
                ins.then_inc(aff_t.sem, 1)
                pe.wait_ge(top_done.sem, top_done.at(l, 0))
                pe.sem_inc(passed["pe"], 1)
                pe.transpose(bank[4][0:CAP, 0:NE], val[:], ident[0:NE, 0:NE])
                pe.transpose(bank[5][0:CAP, 0:NE], idf[:], ident[0:NE, 0:NE]).then_inc(top_t.sem, 1)

                def turn_part(src, h, b, done):
                    for k in range(4):
                        kk = 4 * h + k
                        ins = pe.transpose(bank[b][:, k * CAP:(k + 1) * CAP], src[:, kk * P:(kk + 1) * P], ident[0:CAP, 0:CAP])
                    ins.then_inc(done.sem, 1)

                def turn_xs(e, h):
                    pe.wait_ge(xs_in.sem, xs_in.at(l, e))
                    pe.wait_ge(xs_lo.sem, xs_lo.at(l, 2 * e + (h - 1)))
                    turn_part(XS, h, 7, xs_t)

                turn_xs(0, 0)
                turn_xs(0, 1)

                def expert(e, last):
                    pe.wait_ge(xs_lo.sem, xs_lo.at(l, 2 * e + 1))
                    for pos in range(MPOS):
                        if pos % POOL_EVERY == 0:
                            pe.wait_ge(lo_pool.sem, lo_pool.at(l, e * (MPOS // POOL_EVERY) + pos // POOL_EVERY))
                        else:
                            pe.wait_ge(lo_made.sem, lo_made.at(l, m_lo_index(e, pos)))
                        wh = m_hi(pos).rearrange("p (k n) -> p k n", k=4)
                        wl = m_lo(pos).rearrange("p (k n) -> p k n", k=4)
                        if pos < 8:
                            if pos % 4 == 0:
                                pe.wait_ge(act_ok.sem, act_ok.at(l, 2 * e + (pos // 4 - 2)))
                            out, hi, lo, half = bank[pos // 2][0:CAP, :], xsT_hi, xsT_lo, pos % 2
                        else:
                            i, half = (pos - 8) % 2, (pos - 8) // 2
                            if i == 0:
                                pe.wait_ge(a_lo.sem, a_lo.at(l, 2 * e + half))
                            if half == 0:
                                pe.wait_ge(y_ev.sem, y_ev.at(l, 2 * e + (i - 2)))
                            out, hi, lo = bank[4 + i][0:CAP, :], aT_hi, aT_lo
                        for k in range(4):
                            kk = half * 4 + k
                            ins = product3(out, hi[:, kk, :], lo[:, kk, :], wh[:, k, :], wl[:, k, :],
                                           half == 0 and k == 0, half == 1 and k == 3)
                        ins.then_inc(m_used.sem, 1)
                        if pos in (5, 8):
                            i = pos // 8
                            pe.wait_ge(act_ok.sem, act_ok.at(l, 2 * e + i))
                            pe.wait_ge(a_lo.sem, a_lo.at(l, 2 * e + (i - 1)))
                            turn_part(act_s, i, 6, a_t)
                        if pos in (7, 9) and not last:
                            turn_xs(e + 1, pos // 9)

                with pe.Fori(0, NE - 1) as e:
                    expert(e, False)
                expert(NE - 1, True)


_W = ['w_in', 'b_w_q_b', 'b_w_kv_b', 'w_mem_kv', 'w_branch', 'w_out', 'w_router', 'w_gate_up', 'w_down']
_G = ['norm1_g', 'a_q_norm', 'a_k_norm', 'b_q_a_norm', 'b_kv_a_norm', 'b_q_norm', 'b_k_norm', 'c_q_norm', 'c_k_norm',
      'c_sink', 'x_q_norm', 'x_k_norm', 'mem_norm_g', 'norm2_g']


def shape_tables():
    import numpy as np
    theta, grid_w = np.float32(10000.0), 64

    def angles(pos, dim):
        inv = np.power(theta, -np.arange(0, dim, 2, dtype=np.float32) / np.float32(dim)).astype(np.float32)
        return pos.astype(np.float32)[:, None] * inv[None, :]

    def rotary(ang):
        c, s = np.cos(ang).astype(np.float32), np.sin(ang).astype(np.float32)
        return np.concatenate([c, c], 1), np.concatenate([-s, s], 1)

    pos = np.concatenate([np.arange(n * P) for _, n in SEQS])
    (cr, sr), (cc, sc) = rotary(angles(pos // grid_w, HD // 2)), rotary(angles(pos % grid_w, HD // 2))
    cb, sb_ = rotary(angles(pos, ROPE))

    def tiles(a):
        return np.ascontiguousarray(a.reshape(NT, P, -1).transpose(1, 0, 2))

    cb, sb_ = (np.repeat(tiles(a), 2, axis=1) for a in (cb, sb_))
    dist = np.abs(np.arange(7 * P)[None, :] - 3 * P - np.arange(P)[:, None]).astype(np.float32)
    slopes = np.power(np.float32(2.0), -np.arange(1, 9, dtype=np.float32))
    return {"cosA": tiles(np.concatenate([cr, cc], 1)), "sinA": tiles(np.concatenate([sr, sc], 1)),
            "cosB": np.ascontiguousarray(cb), "sinB": np.ascontiguousarray(sb_),
            "ndist": np.where(dist <= 128, -dist, np.float32(-1e30)).astype(np.float32),
            "slopes": np.ascontiguousarray(np.broadcast_to(slopes, (P, 8)))}


def kernel(**inputs):
    import numpy as _np
    import concourse.bacc as _bacc
    from concourse import mybir as _mybir
    from concourse.bass_utils import run_bass_kernel_spmd as _run

    nc = _bacc.Bacc("TRN2", target_bir_lowering=False, num_devices=1, dynamic_dma_scratch_size=4096)
    arrays = {}

    def give(name, a):
        a = _np.ascontiguousarray(a)
        arrays[f"in_{name}_dram"] = a
        return nc.dram_tensor(f"in_{name}_dram", a.shape, _mybir.dt.from_np(a.dtype), kind="ExternalInput").ap()

    x = give("x", _np.concatenate([inputs["x_prompt"][0], inputs["x_sample"][0]], 0))
    mem = give("mem", _np.concatenate([inputs["mem_prompt"][0], inputs["mem_sample"][0]], 0))
    w = {n: give(n, inputs[n]) for n in _W}
    for n in ("w_gate_up", "w_down"):
        w[n] = w[n].rearrange("l e d f -> (l e) d f")
    g = {n: give(n, inputs[n]) for n in _G}
    tables = {n: give(n, a) for n, a in shape_tables().items()}
    outs = [nc.dram_tensor(f"out_{i}_dram", (1, n * P, D), _mybir.dt.float32, kind="ExternalOutput").ap()
            for i, (_, n) in enumerate(SEQS)]
    build(nc, x, mem, w, g, tables, outs[0][0], outs[1][0])
    r = _run(nc, [arrays], core_ids=[0])
    return tuple(r.results[0][f"out_{i}_dram"] for i in range(2))
```
